# Optimizing a Trainium2 kernel written in Bass

```python
import jax, jax.numpy as jnp
from jax import lax
import numpy as np

D_MODEL = 1024
BATCH = 1
SEQ = 256
DEPTH = 1

CTX_LEN = 256
GRID_W = 64

A_HEADS = 4
A_DK = 128
A_DV = 128
A_KW = A_HEADS * A_DK
A_VW = A_HEADS * A_DV
A_CHUNK = 64

B_GROUPS = 4
B_GW = 128
B_W = B_GROUPS * B_GW
B_CHUNK = 2 * GRID_W

D_FF = -(-8 * D_MODEL // (3 * 256)) * 256

N_MOD = 6
EPS = 1e-6

CTX_STATE_COLS = 2 * A_KW + A_VW
SPLIT_IDX = (A_KW, 2 * A_KW, 2 * A_KW + A_VW, 3 * A_KW + A_VW, 3 * A_KW + 2 * A_VW,
             3 * A_KW + 2 * A_VW + B_W, 3 * A_KW + 2 * A_VW + 2 * B_W,
             3 * A_KW + 2 * A_VW + 2 * B_W + D_MODEL)
IN_COLS = 3 * A_KW + 2 * A_VW + 2 * B_W + 2 * D_MODEL


def rmsnorm(x, g):
    xf = x.astype(jnp.float32)
    y = xf * lax.rsqrt(jnp.mean(xf * xf, axis=-1, keepdims=True) + EPS)
    return (y * g.astype(jnp.float32)).astype(x.dtype)

def layernorm(x, g, b):
    xf = x.astype(jnp.float32)
    mu = jnp.mean(xf, axis=-1, keepdims=True)
    var = jnp.mean(jnp.square(xf - mu), axis=-1, keepdims=True)
    y = (xf - mu) * lax.rsqrt(var + EPS) * g.astype(jnp.float32) + b.astype(jnp.float32)
    return y.astype(x.dtype)

def modulate(h, shift, scale):
    return h * (1 + scale) + shift

def split_heads(t):
    return t.reshape(t.shape[0], t.shape[1], A_HEADS, -1).astype(jnp.float32)

def flip_seq(t):
    return jnp.flip(t, axis=1)

def forget_gate(f_logit, lb):
    f = lb + (1 - lb) * jax.nn.sigmoid(f_logit.astype(jnp.float32))
    return jnp.log(f), 1 - f

def hgrn2_chunked(q, k, logf, v, s0):
    b_, L = q.shape[:2]
    n = L // A_CHUNK
    rs = lambda t: t.reshape(b_, n, A_CHUNK, *t.shape[2:])
    q, k, logf, v = rs(q), rs(k), rs(logf), rs(v)
    bcum = jnp.cumsum(logf, axis=2)
    blast = bcum[:, :, -1:]
    mid = 0.5 * blast
    q_in = q * jnp.exp(bcum - mid)
    k_in = k * jnp.exp(mid - bcum)
    scores = jnp.einsum('bnthd,bnshd->bnhts', q_in, k_in)
    mask = jnp.tril(jnp.ones((A_CHUNK, A_CHUNK), dtype=bool))
    scores = jnp.where(mask, scores, 0.0)
    o_intra = jnp.einsum('bnhts,bnshe->bnthe', scores, v)
    d_state = jnp.einsum('bnshd,bnshe->bnhde', k * jnp.exp(blast - bcum), v)
    decay = jnp.exp(blast[:, :, 0])

    def step(s, inp):
        a, d = inp
        return a[..., None] * s + d, s

    s_final, s_in = lax.scan(step, s0, (jnp.moveaxis(decay, 1, 0), jnp.moveaxis(d_state, 1, 0)))
    s_in = jnp.moveaxis(s_in, 0, 1)
    o_inter = jnp.einsum('bnthd,bnhde->bnthe', q * jnp.exp(bcum), s_in)
    o = (o_intra + o_inter).reshape(b_, L, A_HEADS, A_DV)
    return o, s_final

def hgrn2_final_state(k, logf, v):
    bcum = jnp.cumsum(logf, axis=1)
    w = k * jnp.exp(bcum[:, -1:] - bcum)
    return jnp.einsum('blhd,blhe->bhde', w, v)

def chunk_sgu(u, v, ln_g, ln_b, w_s, b_s, n_chunks):
    b_, L = u.shape[:2]
    v = layernorm(v, ln_g, ln_b)
    vc = v.reshape(b_, n_chunks, B_CHUNK, B_GROUPS, B_GW)
    mixed = jnp.einsum('gts,bnsgc->bntgc', w_s, vc) + jnp.transpose(b_s)[:, :, None]
    return u * mixed.reshape(b_, L, B_W)

def token_mixers(p, lb, g_norm_a, ln_v_g, ln_v_b, w_s, b_s, w_pa, w_pb, w_o, s0_f, s0_b, n_chunks_b):
    f_f, f_b, i_in, q, og, u, v, ga, gb = jnp.split(p, SPLIT_IDX, axis=-1)
    b_, L = p.shape[:2]
    logf_f, k_f = forget_gate(f_f, lb[0])
    logf_b, k_b = forget_gate(f_b, lb[1])
    qh, vh = split_heads(q), split_heads(i_in)
    o_f, s_f = hgrn2_chunked(qh, split_heads(k_f), split_heads(logf_f), vh, s0_f)
    o_b, s_b = hgrn2_chunked(flip_seq(qh), flip_seq(split_heads(k_b)), flip_seq(split_heads(logf_b)),
                             flip_seq(vh), s0_b)
    o_a = rmsnorm(o_f + flip_seq(o_b), g_norm_a).reshape(b_, L, A_VW).astype(p.dtype)
    o_a = o_a * jax.nn.silu(og)
    o_b_mlp = chunk_sgu(jax.nn.gelu(u), jax.nn.gelu(v), ln_v_g, ln_v_b, w_s, b_s, n_chunks_b)
    merged = jax.nn.sigmoid(ga) * (o_a @ w_pa) + jax.nn.sigmoid(gb) * (o_b_mlp @ w_pb)
    return merged @ w_o, s_f, s_b

def swiglu(h, w_up, w_down):
    a, b = jnp.split(h @ w_up, 2, axis=-1)
    return (jax.nn.silu(a) * b) @ w_down

def first_inputs(seed: int = 0) -> dict:
    key = jax.random.key(seed)
    ks = jax.random.split(key, 21)
    nrm = lambda k, shape, s: jax.random.normal(k, shape, jnp.float32) * s
    return {
        'x': nrm(ks[0], (BATCH, SEQ, D_MODEL), 1.0),
        'c': nrm(ks[1], (BATCH, D_MODEL), 1.0),
        'ctx': nrm(ks[2], (BATCH, CTX_LEN, D_MODEL), 1.0),
        'c_ctx': nrm(ks[3], (D_MODEL,), 1.0),
        'w_mod': nrm(ks[4], (DEPTH, D_MODEL, N_MOD * D_MODEL), 0.5 * D_MODEL ** -0.5),
        'b_mod': nrm(ks[5], (DEPTH, N_MOD * D_MODEL), 0.01),
        'g_mix': 1.0 + nrm(ks[6], (DEPTH, D_MODEL), 0.1),
        'g_ffn': 1.0 + nrm(ks[7], (DEPTH, D_MODEL), 0.1),
        'w_in': nrm(ks[8], (DEPTH, D_MODEL, IN_COLS), D_MODEL ** -0.5),
        'lb_gamma': nrm(ks[9], (DEPTH + 1, 2, A_KW), 0.5),
        'g_norm_a': 1.0 + nrm(ks[10], (DEPTH, A_DV), 0.1),
        'ln_v_g': 1.0 + nrm(ks[11], (DEPTH, B_W), 0.1),
        'ln_v_b': nrm(ks[12], (DEPTH, B_W), 0.02),
        'w_s': nrm(ks[13], (DEPTH, B_GROUPS, B_CHUNK, B_CHUNK), 0.5 * B_CHUNK ** -0.5),
        'b_s': 1.0 + nrm(ks[14], (DEPTH, B_GROUPS, B_CHUNK), 0.1),
        'w_pa': nrm(ks[15], (DEPTH, A_VW, D_MODEL), A_VW ** -0.5),
        'w_pb': nrm(ks[16], (DEPTH, B_W, D_MODEL), B_W ** -0.5),
        'w_o': nrm(ks[17], (DEPTH, D_MODEL, D_MODEL), D_MODEL ** -0.5),
        'w_up': nrm(ks[18], (DEPTH, D_MODEL, 2 * D_FF), D_MODEL ** -0.5),
        'w_down': nrm(ks[19], (DEPTH, D_FF, D_MODEL), D_FF ** -0.5),
        'g_final': 1.0 + nrm(ks[20], (D_MODEL,), 0.1),
    }

def first_block(x, c, ctx, c_ctx, w_mod, b_mod, g_mix, g_ffn, w_in, lb_gamma, g_norm_a,
              ln_v_g, ln_v_b, w_s, b_s, w_pa, w_pb, w_o, w_up, w_down, g_final):
    bsz, L = x.shape[0], x.shape[1]
    rows = L // GRID_W
    n_chunks_lat = rows // 2
    n_chunks_ctx = ctx.shape[1] // B_CHUNK
    lb_all = jnp.cumsum(jax.nn.softmax(lb_gamma.astype(jnp.float32), axis=0), axis=0)
    for l in range(DEPTH):
        last = l == DEPTH - 1
        lb = lb_all[l]
        mod = (jax.nn.silu(c) @ w_mod[l] + b_mod[l]).reshape(bsz, N_MOD, D_MODEL)
        mc = (jax.nn.silu(c_ctx) @ w_mod[l] + b_mod[l]).reshape(N_MOD, D_MODEL)
        hc = modulate(rmsnorm(ctx, g_mix[l]), mc[0], mc[1])
        if last:
            pc = hc @ w_in[l][:, :CTX_STATE_COLS]
            f_f, f_b, i_c = jnp.split(pc, (A_KW, 2 * A_KW), axis=-1)
            logf_f, k_f = forget_gate(f_f, lb[0])
            logf_b, k_b = forget_gate(f_b, lb[1])
            vh = split_heads(i_c)
            s_ctx_f = hgrn2_final_state(split_heads(k_f), split_heads(logf_f), vh)
            s_ctx_b = hgrn2_final_state(flip_seq(split_heads(k_b)), flip_seq(split_heads(logf_b)), flip_seq(vh))
        else:
            zeros = jnp.zeros((bsz, A_HEADS, A_DK, A_DV), jnp.float32)
            mix_c, s_ctx_f, s_ctx_b = token_mixers(hc @ w_in[l], lb, g_norm_a[l], ln_v_g[l], ln_v_b[l],
                                                   w_s[l], b_s[l], w_pa[l], w_pb[l], w_o[l],
                                                   zeros, zeros, n_chunks_ctx)
            ctx = ctx + mc[2] * mix_c
            hc2 = modulate(rmsnorm(ctx, g_ffn[l]), mc[3], mc[4])
            ctx = ctx + mc[5] * swiglu(hc2, w_up[l], w_down[l])
        h = modulate(rmsnorm(x, g_mix[l]), mod[:, 0, None], mod[:, 1, None])
        mix_x, _, _ = token_mixers(h @ w_in[l], lb, g_norm_a[l], ln_v_g[l], ln_v_b[l],
                                   w_s[l], b_s[l], w_pa[l], w_pb[l], w_o[l],
                                   s_ctx_f, s_ctx_b, n_chunks_lat)
        x = x + mod[:, 2, None] * mix_x
        h2 = modulate(rmsnorm(x, g_ffn[l]), mod[:, 3, None], mod[:, 4, None])
        x = x + mod[:, 5, None] * swiglu(h2, w_up[l], w_down[l])
    return rmsnorm(x, g_final)


DEPTH_2 = 2

GLA_HEADS = 4
GLA_DK = 128
GLA_DV = 256
GLA_GATE_RANK = 16
GLA_GATE_TAU = 16.0
GLA_CHUNK = 64
GLA_PROJ = GLA_HEADS * (2 * GLA_DK + 2 * GLA_DV) + GLA_GATE_RANK
SWA_HEADS = 16
SWA_KV_HEADS = 4
SWA_GROUP = SWA_HEADS // SWA_KV_HEADS
SWA_HEAD_DIM = 64
SWA_WINDOW = 128
SWA_BLOCK = 128
ROT_DIM = SWA_HEAD_DIM // 4
ROPE_THETA = 500000.0
PEER_HEADS = 8
PEER_N_KEYS = 128
PEER_EXPERTS = PEER_N_KEYS * PEER_N_KEYS
PEER_TOPK = 16
PEER_QDIM = 256
PEER_BLOCK = 128


def rmsnorm_2(x, g):
    x32 = x.astype(jnp.float32)
    y = x32 * lax.rsqrt(jnp.mean(x32 * x32, axis=-1, keepdims=True) + EPS)
    return (y * g.astype(jnp.float32)).astype(x.dtype)

def modulate_2(x, g, shift, scale):
    return rmsnorm_2(x, g) * (1.0 + scale[:, None, :]) + shift[:, None, :]

def rope_tables(positions):
    inv = ROPE_THETA ** (-jnp.arange(0, ROT_DIM, 2, dtype=jnp.float32) / ROT_DIM)
    ang = positions.astype(jnp.float32)[..., None] * inv
    return jnp.cos(ang), jnp.sin(ang)

def apply_partial_rope(x, cos, sin):
    half = ROT_DIM // 2
    xr = x[..., :ROT_DIM].astype(jnp.float32)
    x1, x2 = xr[..., :half], xr[..., half:]
    c = cos[:, :, None, :]
    s = sin[:, :, None, :]
    rot = jnp.concatenate([x1 * c - x2 * s, x2 * c + x1 * s], axis=-1).astype(x.dtype)
    return jnp.concatenate([rot, x[..., ROT_DIM:]], axis=-1)

def gla_mixer(h, w_in, w_g2, b_g2, norm_g, w_out):
    bsz, s_len, _ = h.shape
    H, dk, dv, C = GLA_HEADS, GLA_DK, GLA_DV, GLA_CHUNK
    n_c = s_len // C
    proj = h @ w_in
    q, k, v, og, gl = jnp.split(proj, [H * dk, 2 * H * dk, 2 * H * dk + H * dv, 2 * H * dk + 2 * H * dv], axis=-1)
    log_a = jax.nn.log_sigmoid((gl @ w_g2 + b_g2).astype(jnp.float32)) / GLA_GATE_TAU
    shp = (bsz, n_c, C, H, dk)
    q = q.reshape(shp).astype(jnp.float32) * (dk ** -0.5)
    k = k.reshape(shp).astype(jnp.float32)
    v = v.reshape(bsz, n_c, C, H, dv).astype(jnp.float32)
    b = jnp.cumsum(log_a.reshape(shp), axis=2)
    b_last = b[:, :, -1:]
    q_t = q * jnp.exp(b)
    k_t = k * jnp.exp(-b)
    k_dec = k * jnp.exp(b_last - b)
    scores = jnp.einsum('bnchd,bnmhd->bnhcm', q_t, k_t)
    tri = jnp.tril(jnp.ones((C, C), dtype=bool))
    scores = jnp.where(tri, scores, 0.0)
    o_intra = jnp.einsum('bnhcm,bnmhe->bnche', scores, v)
    dec = jnp.exp(b_last[:, :, 0])

    def step(state, inp):
        q_n, k_n, v_n, d_n = inp
        o_n = jnp.einsum('bchd,bhde->bche', q_n, state)
        state = d_n[..., None] * state + jnp.einsum('bchd,bche->bhde', k_n, v_n)
        return state, o_n

    xs = (jnp.moveaxis(q_t, 1, 0), jnp.moveaxis(k_dec, 1, 0), jnp.moveaxis(v, 1, 0), jnp.moveaxis(dec, 1, 0))
    _, o_inter = lax.scan(step, jnp.zeros((bsz, H, dk, dv), jnp.float32), xs)
    o = (o_intra + jnp.moveaxis(o_inter, 0, 1)).reshape(bsz, s_len, H, dv)
    o = rmsnorm_2(o, norm_g) * jax.nn.silu(og.reshape(bsz, s_len, H, dv).astype(jnp.float32))
    return (o.reshape(bsz, s_len, H * dv) @ w_out).astype(h.dtype)

def shared_kv(h, kv_w, cos, sin):
    bsz, s_len, _ = h.shape
    kv = h @ kv_w
    k, v = jnp.split(kv, 2, axis=-1)
    k = apply_partial_rope(k.reshape(bsz, s_len, SWA_KV_HEADS, SWA_HEAD_DIM), cos, sin)
    v = v.reshape(bsz, s_len, SWA_KV_HEADS, SWA_HEAD_DIM)
    return k, v

def swa_sink_attention(h, w_q, sinks, w_out, k, v, cos, sin):
    bsz, s_len, _ = h.shape
    P = SWA_BLOCK
    n_b = s_len // P
    q = apply_partial_rope((h @ w_q).reshape(bsz, s_len, SWA_HEADS, SWA_HEAD_DIM), cos, sin)
    q = q.reshape(bsz, n_b, P, SWA_KV_HEADS, SWA_GROUP, SWA_HEAD_DIM)

    def band(t):
        prev = jnp.pad(t, ((0, 0), (P, 0), (0, 0), (0, 0)))[:, :s_len]
        shp = (bsz, n_b, P, SWA_KV_HEADS, SWA_HEAD_DIM)
        return jnp.concatenate([prev.reshape(shp), t.reshape(shp)], axis=2)

    k_band, v_band = band(k), band(v)
    s = jnp.einsum('bnqkgd,bnmkd->bnkgqm', q, k_band).astype(jnp.float32) * (SWA_HEAD_DIM ** -0.5)
    qi = jnp.arange(P)[:, None]
    mi = jnp.arange(2 * P)[None, :]
    rel = qi + P - mi
    in_window = (rel >= 0) & (rel < SWA_WINDOW)
    key_pos = jnp.arange(n_b)[:, None, None] * P - P + mi[None]
    mask = in_window[None] & (key_pos >= 0)
    s = jnp.where(mask[None, :, None, None], s, -jnp.inf)
    sink = sinks.astype(jnp.float32).reshape(SWA_KV_HEADS, SWA_GROUP)[None, None, :, :, None, None]
    m = jnp.maximum(jnp.max(s, axis=-1, keepdims=True), sink)
    p = jnp.exp(s - m)
    probs = p / (jnp.sum(p, axis=-1, keepdims=True) + jnp.exp(sink - m))
    o = jnp.einsum('bnkgqm,bnmkd->bnqkgd', probs, v_band.astype(jnp.float32))
    return (o.reshape(bsz, s_len, SWA_HEADS * SWA_HEAD_DIM) @ w_out).astype(h.dtype)

def peer(h, w_q, subkeys, u_tab, v_tab):
    bsz, s_len, d = h.shape
    half = PEER_QDIM // 2
    tokens = h.reshape(-1, PEER_BLOCK, d)

    def block(xb):
        q = (xb @ w_q).reshape(PEER_BLOCK, PEER_HEADS, PEER_QDIM)
        s1 = jnp.einsum('phd,nd->phn', q[..., :half], subkeys[0])
        s2 = jnp.einsum('phd,nd->phn', q[..., half:], subkeys[1])
        v1, i1 = lax.top_k(s1, PEER_TOPK)
        v2, i2 = lax.top_k(s2, PEER_TOPK)
        cand = (v1[..., :, None] + v2[..., None, :]).reshape(PEER_BLOCK, PEER_HEADS, PEER_TOPK * PEER_TOPK)
        cs, ci = lax.top_k(cand, PEER_TOPK)
        e = (jnp.take_along_axis(i1, ci // PEER_TOPK, axis=-1) * PEER_N_KEYS
             + jnp.take_along_axis(i2, ci % PEER_TOPK, axis=-1))
        g = jax.nn.softmax(cs.astype(jnp.float32), axis=-1)
        u = u_tab[e]
        a = jax.nn.gelu(jnp.einsum('pd,phkd->phk', xb, u).astype(jnp.float32), approximate=False)
        return jnp.einsum('phk,phkd->pd', g * a, v_tab[e].astype(jnp.float32)).astype(xb.dtype)

    return lax.map(block, tokens).reshape(bsz, s_len, d)

def second_inputs(seed: int = 0) -> dict:
    key = jax.random.key(seed)
    ks = jax.random.split(key, 24)
    n_a = DEPTH_2 // 2
    n_b = DEPTH_2 - n_a
    D = D_MODEL
    f32 = jnp.float32

    def nrm(k, shape, scale):
        return jax.random.normal(k, shape, f32) * scale

    positions = (jax.random.randint(ks[2], (BATCH, 1), 0, 4096, dtype=jnp.int32)
                 + jnp.arange(SEQ, dtype=jnp.int32)[None, :])
    return {
        "x": nrm(ks[0], (BATCH, SEQ, D), 1.0),
        "c": nrm(ks[1], (BATCH, D), 1.0),
        "positions": positions,
        "mod_w": nrm(ks[3], (DEPTH_2, D, 6 * D), 0.5 * D ** -0.5),
        "mod_b": nrm(ks[4], (DEPTH_2, 6 * D), 0.02),
        "norm_g": 1.0 + nrm(ks[5], (DEPTH_2, 2, D), 0.02),
        "gla_w_in": nrm(ks[6], (n_a, D, GLA_PROJ), D ** -0.5),
        "gla_w_g2": nrm(ks[7], (n_a, GLA_GATE_RANK, GLA_HEADS * GLA_DK), GLA_GATE_RANK ** -0.5),
        "gla_b_g2": nrm(ks[8], (n_a, GLA_HEADS * GLA_DK), 0.1),
        "gla_norm_g": 1.0 + nrm(ks[9], (n_a, GLA_DV), 0.02),
        "gla_w_out": nrm(ks[10], (n_a, GLA_HEADS * GLA_DV, D), (GLA_HEADS * GLA_DV) ** -0.5),
        "kv_mod_w": nrm(ks[11], (D, 2 * D), 0.5 * D ** -0.5),
        "kv_mod_b": nrm(ks[12], (2 * D,), 0.02),
        "kv_norm_g": 1.0 + nrm(ks[13], (D,), 0.02),
        "kv_w": nrm(ks[14], (D, 2 * SWA_KV_HEADS * SWA_HEAD_DIM), D ** -0.5),
        "swa_w_q": nrm(ks[15], (n_b, D, SWA_HEADS * SWA_HEAD_DIM), D ** -0.5),
        "swa_sinks": nrm(ks[16], (n_b, SWA_HEADS), 0.5),
        "swa_w_out": nrm(ks[17], (n_b, SWA_HEADS * SWA_HEAD_DIM, D), (SWA_HEADS * SWA_HEAD_DIM) ** -0.5),
        "peer_w_q": nrm(ks[18], (DEPTH_2, D, PEER_HEADS * PEER_QDIM), D ** -0.5),
        "peer_subkeys": nrm(ks[19], (DEPTH_2, 2, PEER_N_KEYS, PEER_QDIM // 2), (PEER_QDIM // 2) ** -0.5),
        "peer_u": nrm(ks[20], (DEPTH_2, PEER_EXPERTS, D), D ** -0.5),
        "peer_v": nrm(ks[21], (DEPTH_2, PEER_EXPERTS, D), PEER_HEADS ** -0.5),
        "final_norm_g": 1.0 + nrm(ks[22], (D,), 0.02),
    }

def second_block(x, c, positions, mod_w, mod_b, norm_g, gla_w_in, gla_w_g2, gla_b_g2, gla_norm_g,
              gla_w_out, kv_mod_w, kv_mod_b, kv_norm_g, kv_w, swa_w_q, swa_sinks, swa_w_out,
              peer_w_q, peer_subkeys, peer_u, peer_v, final_norm_g):
    n_a = DEPTH_2 // 2
    cos, sin = rope_tables(positions)
    c_act = jax.nn.silu(c)
    k_sh, v_sh = None, None
    for l in range(DEPTH_2):
        mod = c_act @ mod_w[l] + mod_b[l]
        sh1, sc1, g1, sh2, sc2, g2 = jnp.split(mod, 6, axis=-1)
        h = modulate_2(x, norm_g[l, 0], sh1, sc1)
        if l < n_a:
            y = gla_mixer(h, gla_w_in[l], gla_w_g2[l], gla_b_g2[l], gla_norm_g[l], gla_w_out[l])
        else:
            j = l - n_a
            y = swa_sink_attention(h, swa_w_q[j], swa_sinks[j], swa_w_out[j], k_sh, v_sh, cos, sin)
        x = x + (g1[:, None, :] * y).astype(x.dtype)
        h = modulate_2(x, norm_g[l, 1], sh2, sc2)
        y = peer(h, peer_w_q[l], peer_subkeys[l], peer_u[l], peer_v[l])
        x = x + (g2[:, None, :] * y).astype(x.dtype)
        if l == n_a - 1:
            kv_mod = c_act @ kv_mod_w + kv_mod_b
            kv_shift, kv_scale = jnp.split(kv_mod, 2, axis=-1)
            k_sh, v_sh = shared_kv(modulate_2(x, kv_norm_g, kv_shift, kv_scale), kv_w, cos, sin)
    return rmsnorm_2(x, final_norm_g)


def setup_inputs(seed=0):
    out = dict(first_inputs(seed))
    for name, value in second_inputs(seed + 1).items():
        if name != "x":
            out[name + "_2"] = value
    return out


def reference(
    x, c, ctx, c_ctx, w_mod, b_mod, g_mix, g_ffn, w_in, lb_gamma, g_norm_a, ln_v_g, ln_v_b, w_s,
    b_s, w_pa, w_pb, w_o, w_up, w_down, g_final, c_2, positions_2, mod_w_2, mod_b_2, norm_g_2,
    gla_w_in_2, gla_w_g2_2, gla_b_g2_2, gla_norm_g_2, gla_w_out_2, kv_mod_w_2, kv_mod_b_2,
    kv_norm_g_2, kv_w_2, swa_w_q_2, swa_sinks_2, swa_w_out_2, peer_w_q_2, peer_subkeys_2,
    peer_u_2, peer_v_2, final_norm_g_2,
):
    x = first_block(
        x, c, ctx, c_ctx, w_mod, b_mod, g_mix, g_ffn, w_in, lb_gamma, g_norm_a, ln_v_g, ln_v_b,
        w_s, b_s, w_pa, w_pb, w_o, w_up, w_down, g_final,
    )
    return second_block(
        x, c_2, positions_2, mod_w_2, mod_b_2, norm_g_2, gla_w_in_2, gla_w_g2_2, gla_b_g2_2,
        gla_norm_g_2, gla_w_out_2, kv_mod_w_2, kv_mod_b_2, kv_norm_g_2, kv_w_2, swa_w_q_2,
        swa_sinks_2, swa_w_out_2, peer_w_q_2, peer_subkeys_2, peer_u_2, peer_v_2,
        final_norm_g_2,
    )


_drawn_inputs = setup_inputs


def setup_inputs(seed=0):
    import zlib

    import numpy as np

    out = dict(_drawn_inputs(seed))
    spreads = {}
    factors = {'ctx': 6.684,
     'c_ctx': 8.0,
     'b_mod': 3.808,
     'g_norm_a': 3.344,
     'ln_v_g': 5.54,
     'ln_v_b': 8.0,
     'b_s': 3.652,
     'norm_g_2': 3.778,
     'gla_b_g2_2': 4.394,
     'gla_norm_g_2': 7.933,
     'kv_mod_b_2': 6.692,
     'kv_norm_g_2': 8.0,
     'swa_sinks_2': 64.0,
     'final_norm_g_2': 8.841}
    for name, (base, spread) in spreads.items():
        noise = np.random.default_rng([zlib.crc32(name.encode()), seed]).standard_normal(out[name].shape)
        drawn = base * np.exp(spread * noise) if base else spread * noise
        out[name] = __import__('jax').numpy.asarray(drawn.astype(out[name].dtype))
    for name, factor in factors.items():
        out[name] = (out[name] * factor).astype(out[name].dtype)
    return out
```

```python
from contextlib import ExitStack

import numpy as np
from concourse import bass, mybir

D, T, P, KT = 1024, 256, 128, 8
FF = 2816
FT = FF // P
HEADS, CHUNK, NCH = 4, 64, 4
RING = 4
SLOT = 2048
EXPERTS, PH, TOPK = 16384, 8, 16
EPS = 1e-6

VEC_SIZES = [("c", 8), ("c_ctx", 8), ("c_2", 8), ("b_mod", 48), ("g_mix", 8), ("g_ffn", 8), ("g_final", 8),
             ("lb_gamma", 16), ("g_norm_a", 1), ("mod_b_2", 96), ("norm_g_2", 32), ("gla_b_g2", 4),
             ("gla_norm_g", 2), ("kv_mod_b", 16), ("kv_norm_g", 8), ("final_norm_g", 8),
             ("sinks", 16)]
VEC, _n = {}, 0
for _name, _size in VEC_SIZES:
    VEC[_name] = (_n, _n + _size)
    _n += _size
VEC_COLS = _n
CONST_SIZES = [("ident", 128), ("ones", 128), ("iota", 128), ("rot", 128), ("scan_g", 256), ("inv_freq", 1), ("half_pi", 1)]
CON, _n = {}, 0
for _name, _size in CONST_SIZES:
    CON[_name] = (_n, _n + _size)
    _n += _size
CON_COLS = _n
MIX_SIZES = [("scan_f", 512), ("scan_b", 512), ("ln_v_g", 512), ("ln_v_b", 512), ("b_s", 512)]


class Counts:

    def __init__(self, sems):
        self.sems = sems
        self.seen, self.fills, self.tile, self.steps = {}, {}, 0, 0
        self.i, self.rates = None, {}

    def value(self, name, n):
        return n if self.i is None or name not in self.rates else n + self.i * self.rates[name]

    def skip(self, name, n):
        self.seen[name] = self.seen.get(name, 0) + n

    def more(self, name, n=1):
        self.skip(name, n)
        return self.value(name, self.seen[name])

    def refill(self, name):
        self.fills[name] = self.fills.get(name, 0) + 1
        return self.fills[name] > 1

    def freed(self, name):
        return self.value(name, self.fills[name] - 1)

    def stepped(self):
        self.steps += 1
        return self.value("dve_step", self.steps)

    def tiles(self, name, n):
        self.tile += n
        self.skip(name, n)

    def tile_out(self, back=1):
        n = self.tile - back
        name = f"bank{4 + n % 2}"
        return self.sems[name], self.value(name, n // 2 + 1)

    def loop(self, i, rates):
        self.i, self.rates = i, rates

    def end_loop(self, times):
        for name, rate in self.rates.items():
            if name == "dve_step":
                self.steps += rate * (times - 1)
            if name in self.seen:
                self.seen[name] += rate * (times - 1)
            if name in self.fills:
                self.fills[name] += rate * (times - 1)
        self.i, self.rates = None, {}


def build(nc, a, out):
    f32, u32, i32 = mybir.dt.float32, mybir.dt.uint32, mybir.dt.int32
    ALU, ACT, AX = mybir.AluOpType, mybir.ActivationFunctionType, mybir.AxisListType
    MUL, ADD, SUB = ALU.mult, ALU.add, ALU.subtract
    ctx = ExitStack()
    with ctx:
        def sb(name, shape, dt=f32):
            return ctx.enter_context(nc.sbuf_tensor(name, shape, dt))

        xT = sb("xT", [P, KT, T])
        ctxT = sb("ctxT", [P, KT, T])
        H = sb("H", [P, KT, 2 * T])
        ring = sb("ring", [P, RING, SLOT])
        vec = sb("vec", [P, VEC_COLS])
        con = sb("con", [P, CON_COLS])
        masks = sb("masks", [P, 2, 2, CHUNK], i32)
        small = sb("small", [P, 768])
        wsT = small[:, 0:512].rearrange("p (g t) -> p g t", g=4)
        subT = small[:, 512:768].rearrange("p (s n) -> p s n", s=2)
        modc = sb("modc", [P, 64])
        cact = sb("cact", [P, 24])
        gain = sb("gain", [P, 2, 8])
        lbs = sb("lbs", [P, 2, 8])
        nrm = sb("nrm", [P, 2, T])
        macc = sb("macc", [P, 3, T])
        arena = sb("arena", [P, 32768])

        def V(name):
            return vec[:, VEC[name][0]:VEC[name][1]]

        def C(name):
            return con[:, CON[name][0]:CON[name][1]]

        def slot(n):
            return ring[:, n % RING, :]

        def cut(sizes):
            at, views = 0, {}
            for name, size in sizes:
                views[name] = arena[:, at:at + size]
                at += size
            assert at <= 32768, at
            return views

        def kt(ap, k=KT):
            return ap.rearrange("p (k t) -> p k t", k=k)

        hT = H[:, :, :].rearrange("p k t -> p (k t)")[:, 0:KT * T].rearrange("p (k t) -> p k t", k=KT)
        h2nd = H[:, :, :].rearrange("p k t -> p (k t)")[:, KT * T:2 * KT * T]
        Hc, Hx = H[:, :, 0:T], H[:, :, T:2 * T]
        ident, ones, iota = C("ident"), C("ones"), C("iota")
        BK = [ctx.enter_context(nc.psum_tensor(f"bank{i}", [P, 512], f32)) for i in range(8)]

        NAMES = (["consts_in", "x_in", "sub_in", "wgl_in", "pos_in", "wg2_in", "cact", "act_step", "dve_step", "pool_step", "mod_acc",
                  "mod_step", "mod_turn", "mod_bank", "proj", "turn", "bank4", "bank5", "sq", "ms", "var", "std", "h",
                  "lb", "gate", "gates_f", "logf", "expo", "exps", "lin_in", "kturn", "scores", "masked", "scores_free",
                  "dstate", "state", "dstate_free", "o_sum", "o_bank0", "o_bank1", "o_out", "osq", "oms", "ovar", "ostd",
                  "o_done", "wctx", "wctx_in", "s0", "s0_in", "vproj", "vln", "mixed", "mixed_free", "sgu", "merged", 
                  "rows", "y_out", "y_in", "out_done", "final", "gl", "glc", "sp_a", "sp_b", "sp_c",
                  "trig", "roped", "rope_in", "kv_ready", "att_s", "att_max", "att_exp", "att_p", "att_pt", "att_o", "att_bank0", "att_bank1",
                  "q_ready", "peer_top", "peer_sm", "peer_ex", "routes", "routes_in", "p2", "p_free", "g_mm", "g_bank0", "g_bank1",
                  "gelu", "w_ready", "w_free0", "w_free1", "zeroed", "vpad", "att_sfree", "hs", "x_new", "vvar", "vstd", "modulated", "wexp", "cums", "zeroed2", "xexp", "zexp", "zln", "att_sum"]
                 + [f"loaded{i}" for i in range(RING)])
        sems = {n: ctx.enter_context(nc.semaphore(n)) for n in NAMES}
        block = ctx.enter_context(nc.Block())

        M1 = cut([("fg0", 2048), ("fg1", 2048), ("cum0", 2048), ("cum1", 2048),
                  ("qi0", 1024), ("qi1", 1024), ("ki0", 1024), ("ki1", 1024), ("qd0", 1024), ("qd1", 1024),
                  ("kd0", 1024), ("kd1", 1024), ("tA", 1024), ("tB", 1024), ("q", 1024), ("og", 1024), ("u", 1024),
                  ("vN", 2048), ("vS", 1024), ("sc", 1024), ("kN", 512), ("St", 1536), ("S0", 1024),
                  ("oT", 1024), ("dec", 32), ("stat", 32)] + MIX_SIZES)
        mix_in = arena[:, 31808 - 2048:31808 - 2048 + 2560]
        W_ = {0: M1["qi0"], 1: M1["qi1"]}
        M2 = cut([("hf", FT * T), ("sil", 1024), ("yN", 2048)])
        M3 = cut([("cum0", 1024), ("qi0", 1024), ("ki0", 1024), ("kd0", 1024), ("tA", 1024), ("q", 1024), ("k", 1024),
                  ("og", 2048), ("vN", 2048), ("sc", 1024), ("kN", 512), ("St", 1536), ("oT", 2048), ("dec", 32),
                  ("glT", 256), ("zA", 1024), ("zB", 1024), ("wg2", 512), ("osq", 2048), ("wgl", 128)])
        wgl = M3["wgl"].rearrange("p (k r) -> p k r", k=8)
        M4 = cut([("kS", 1024), ("vS", 512), ("vP", 2048), ("cosT", 256), ("sinT", 256), ("qS", 2048), ("tR", 512),
                  ("sS", 768), ("pS", 768), ("pT", 768), ("oS", 2048), ("am", 64), ("ang", 1024), ("pos", 256), ("band", 384)])
        M5 = cut([("qT", 4096), ("s2", 256), ("topv", 512), ("topi", 512), ("topif", 512), ("cand", 256), ("cand2", 256),
                  ("cv", 256), ("ci", 256), ("ca", 256), ("cb", 256), ("caf", 256), ("cbf", 256), ("sel", 768),
                  ("eq", 2048), ("sm", 64)])
        G = arena[:, :].rearrange("p (i t) -> p i t", i=P)
        yN = arena[:, 0:2048].rearrange("p (a d) -> p a d", a=2)
        cflat = ctxT[:, :, :].rearrange("p k t -> p (k t)")
        routes = cflat[:, 0:768].rearrange("p (r t) -> p r t", r=3)
        gelu_t = cflat[:, 768:1280].rearrange("p (b t) -> p b t", b=2)
        w_t = cflat[:, 1280:1792].rearrange("p (b t) -> p b t", b=2)
        P1 = h2nd[:, 0:1024].rearrange("p (b j n) -> p b j n", b=2, j=4)
        P2 = h2nd[:, 1024:2048].rearrange("p (b j n) -> p b j n", b=2, j=4)

        def kview(m, h, d, dirs):
            v = m["kN"][:, 0:512].rearrange("p (d t n) -> p d t n", d=2, t=2)
            return v[:, d if dirs == 2 else h % 2, :, :]

        def state(m, h, d, r, dirs, E):
            v = m["St"].rearrange("p (b r n) -> p b r n", b=4 if dirs == 2 else 2, r=3)
            return v[:, (2 * d + h % 2) if dirs == 2 else h % 2, r, :]

        def chunks(ap, k=4):
            return ap.rearrange("p (h c t) -> p h c t", h=k, c=NCH)

        def xpart(cum):
            return cum.rearrange("p (h s t) -> p h s t", h=4, s=2 * NCH)[:, :, NCH:2 * NCH, :]

        fg = [M1["fg0"].rearrange("p (h t) -> p h t", h=4), M1["fg1"].rearrange("p (h t) -> p h t", h=4)]
        cum = [M1["cum0"].rearrange("p (h t) -> p h t", h=4), M1["cum1"].rearrange("p (h t) -> p h t", h=4)]

        def peer_sections(l):
            return [(a["peer_wq"][l], 8, "proj", 2), ((a["peer_u"][l], a["peer_v"][l]), 128, None, 0)]

        SECTIONS = ([(a["w_mod"], 24, "mod_acc", 1), (a["w_in"], 4, "proj", 2), (a["w_in"], 2, "proj", 4),
                     (a["w_in"], 6, "proj", 2), (a["w_in"], 2, "proj", 2), (a["w_in"], 8, "proj", 2),
                     (a["w_pab"], 4, "proj", 4), (a["w_o"], 4, "proj", 2), (a["w_up"], 22, "proj", 2),
                     (a["w_down"], 11, "rows", 1), (a["mod_w0"], 24, "mod_acc", 1),
                     (a["gla_qk"], 4, "proj", 2), (a["gla_v"], 4, "proj", 2), (a["gla_og"], 4, "proj", 2),
                     (a["gla_out"], 4, "proj", 2)]
                    + peer_sections(0)
                    + [(a["kv_mod"], 8, "mod_acc", 1), (a["kv_k"], 2, "proj", 2), (a["kv_v"], 1, "proj", 2),
                       (a["mod_w1"], 24, "mod_acc", 1), (a["swa_q"], 4, "proj", 2), (a["swa_out"], 4, "proj", 2)]
                    + peer_sections(1))

        @block.sync
        def _(sync):
            e = Counts(sems)
            sync.dma_start(vec[:, :], a["vec"]).then_inc(sems["consts_in"], 16)
            sync.dma_start(con[:, :], a["con"]).then_inc(sems["consts_in"], 16)
            sync.dma_start(masks[:, :, :, :], a["masks"]).then_inc(sems["consts_in"], 16)
            sync.dma_start(xT[:, :, :], a["xT"]).then_inc(sems["x_in"], 16)
            sync.dma_start(ctxT[:, :, :], a["ctxT"]).then_inc(sems["x_in"], 16)
            sync.dma_start(wsT, a["wsT"]).then_inc(sems["x_in"], 16)
            sync.dma_start(mix_in, a["mix"]).then_inc(sems["x_in"], 16)
            n, freed = 0, []
            total = {"proj": 0, "mod_acc": 0, "rows": 0}
            at = {}

            def load(src):
                nonlocal n
                if n >= RING:
                    sync.wait_ge(sems[freed[n - RING][0]], freed[n - RING][1])
                sync.dma_start(slot(n), src).then_inc(sems[f"loaded{n % RING}"], 16)
                n += 1

            for dram, panels, signal, per in SECTIONS:
                if signal is not None:
                    k0 = at.get(id(dram), 0)
                    at[id(dram)] = k0 + panels
                    for k in range(panels):
                        total[signal] += per
                        freed.append((signal, total[signal]))
                        load(dram[k0 + k])
                    continue
                u, v = dram
                for k in range(RING // 2):
                    load(u[k])
                    load(v[k])
                    freed.append(("proj", total["proj"] + 2 * k + 2))
                    freed.append(("rows", total["rows"] + k + 1))
                per_i = RING // 2
                times = 64 // per_i - 1
                with sync.Fori(0, times) as i:
                    for k in range(per_i):
                        sync.wait_ge(sems["proj"], total["proj"] + 2 * k + 2 + i * (2 * per_i))
                        sync.dma_start(slot(n + 2 * k), u[per_i * i + per_i + k]).then_inc(
                            sems[f"loaded{(n + 2 * k) % RING}"], 16)
                        sync.wait_ge(sems["rows"], total["rows"] + k + 1 + i * per_i)
                        sync.dma_start(slot(n + 2 * k + 1), v[per_i * i + per_i + k]).then_inc(
                            sems[f"loaded{(n + 2 * k + 1) % RING}"], 16)
                n += 2 * per_i * times
                total["proj"] += 128
                total["rows"] += 64
                freed += [None] * (n - RING - len(freed))
                for k in range(per_i):
                    freed.append(("proj", total["proj"] - 2 * per_i + 2 * k + 2))
                    freed.append(("rows", total["rows"] - per_i + k + 1))
            sync.wait_ge(sems["out_done"], 16)

        @block.tensor
        def _(pe):
            e = Counts(sems)
            mm = pe.matmul
            panel = [0]

            def next_panel():
                n = panel[0]
                pe.wait_ge(sems[f"loaded{n % RING}"], e.more(f"loaded{n % RING}", 16))
                panel[0] += 1
                return slot(n)

            def ring_bank():
                b = 4 + e.tile % 2
                if e.refill(f"bank{b}"):
                    pe.wait_ge(sems[f"bank{b}"], e.freed(f"bank{b}"))
                e.tile += 1
                return BK[b]

            def mod_stage(panels, ctx_panels=0):
                if e.refill("mod_bank"):
                    pe.wait_ge(sems["mod_bank"], e.freed("mod_bank"))

                def body(n, with_ctx):
                    for r in range(RING):
                        pe.wait_ge(sems["mod_acc"], e.more("mod_acc"))
                        for j in range(2):
                            c = (n + r) * 2 + j
                            last = mm(BK[6][:, bass.ds(c, 1)], macc[:, r % 2, j * P:(j + 1) * P], ones[:, 0:1], start=True, stop=True)
                        if with_ctx:
                            for j in range(2):
                                c = 48 + 2 * (n + r) + j
                                last = mm(BK[6][:, c:c + 1], macc[:, 2, j * P:(j + 1) * P], ones[:, 0:1], start=True, stop=True)
                        last.then_inc(sems["mod_turn"], 1)
                for n in range(0, ctx_panels, RING):
                    body(n, True)
                times = (panels - ctx_panels) // RING
                with pe.Fori(0, times) as i:
                    e.loop(i, {"mod_acc": RING})
                    body(i * RING + ctx_panels, False)
                    e.end_loop(times)
                panel[0] += panels
                for r in range(RING):
                    e.skip(f"loaded{r}", 16 * panels // RING)

            def norm(src):
                for k in range(KT):
                    pe.wait_ge(sems["sq"], e.more("sq"))
                    if k == 0:
                        if e.refill("var"):
                            pe.wait_ge(sems["var"], e.freed("var"))
                    last = mm(BK[7][:, 0:T], ones, src[:, k, :], start=(k == 0), stop=(k == KT - 1))
                last.then_inc(sems["ms"], 1)

            def proj_cols(panels, rhs, width, ks=KT, tiles=2, cols=P):
                for _ in range(panels):
                    w = next_panel().rearrange("p (k c) -> p k c", k=ks)
                    for j in range(tiles):
                        bank = ring_bank()
                        for k in range(ks):
                            last = mm(bank[:, 0:width], w[:, k, j * P:(j + 1) * P], rhs(k), start=(k == 0), stop=(k == ks - 1))
                        last.then_inc(sems["proj"], 1)

            def proj_rows(panels, lhs, tts):
                for _ in range(panels):
                    w = next_panel().rearrange("p (k c) -> p k c", k=KT)
                    for tt in range(tts):
                        bank = ring_bank()
                        for k in range(KT):
                            last = mm(bank[:, 0:2 * P], lhs(k, tt), w[:, k, :], start=(k == 0), stop=(k == KT - 1))
                        last.then_inc(sems["proj"], 1)

            def turn(src_list):
                bank = ring_bank()
                for n, s in enumerate(src_list):
                    last = pe.transpose(bank[:, n * P:(n + 1) * P], s, ident)
                last.then_inc(sems["turn"], 1)

            def lin_pre(m, h, dirs, E, vcols):
                for d in range(dirs):
                    kd = kt(m[f"kd{d}"], 4)
                    turn([kd[:, h, 0:P], kd[:, h, P:2 * P]])
                for d in range(dirs):
                    qi, ki = kt(m[f"qi{d}"], 4), kt(m[f"ki{d}"], 4)
                    for c in range(NCH):
                        tt, hf = c // 2, c % 2
                        s = slice(c * CHUNK, (c + 1) * CHUNK)
                        col = (2 * d + tt) * P + CHUNK * hf
                        last = mm(BK[h % 2][CHUNK * hf:CHUNK * hf + CHUNK, col:col + CHUNK], ki[:, h, s], qi[:, h, s],
                                  start=True, stop=True)
                last.then_inc(sems["scores"], 1)
                for d in range(dirs):
                    pe.wait_ge(*e.tile_out(dirs - d))
                    if e.refill("state"):
                        pe.wait_ge(sems["state"], e.freed("state"))
                    for r in range(3):
                        c = r if d == 0 else NCH - 1 - r
                        tt, hf = c // 2, c % 2
                        rows = slice(CHUNK * hf, CHUNK * hf + CHUNK)
                        b, col = BK[6 + c % 2], c // 2 * E * P
                        last = mm(b[:, col:col + E * P], kview(m, h, d, dirs)[rows, tt, :], vcols(tt, h)[rows, :],
                                  start=True, stop=True)
                    last.then_inc(sems["dstate"], 1)

            def lin_out(m, h, dirs, E, vcols, s0):
                pe.wait_ge(sems["masked"], e.more("masked"))
                if e.refill(f"o_bank{h % 2}"):
                    pe.wait_ge(sems[f"o_bank{h % 2}"], e.freed(f"o_bank{h % 2}"))
                o = BK[2 + h % 2]
                sc = m["sc"].rearrange("p (b q n) -> p b q n", b=2, q=4)
                first = True
                for x in range(E):
                    for d in range(dirs):
                        for tt in range(2):
                            mm(o[:, x * T + tt * P:x * T + tt * P + P], vcols(tt, h)[:, x * P:(x + 1) * P],
                               sc[:, h % 2, 2 * d + tt, :], start=first, stop=False, skip_group_check=True)
                            first = False
                for d in range(dirs):
                    pe.wait_ge(sems["state"], e.more("state"))
                last = None
                for x in range(E):
                    for d in range(dirs):
                        qd = kt(m[f"qd{d}"] if dirs == 2 else m["qi0"], 4)
                        for r in range(NCH):
                            c = r if d == 0 else NCH - 1 - r
                            if r == 0:
                                if s0 is None:
                                    continue
                                st = s0(d, h)
                            else:
                                st = state(m, h, d, r - 1, dirs, E)
                            last = mm(o[:, x * T + c * CHUNK:x * T + (c + 1) * CHUNK], st[:, x * P:(x + 1) * P],
                                      qd[:, h, c * CHUNK:(c + 1) * CHUNK], start=False, stop=(r == NCH - 1),
                                      skip_group_check=True)
                last.then_inc(sems["o_sum"], 1)

            def lin(m, dirs, E, vcols, s0):
                pe.wait_ge(sems["lin_in"], e.more("lin_in"))
                lin_pre(m, 0, dirs, E, vcols)
                for h in range(HEADS):
                    if h + 1 < HEADS:
                        lin_pre(m, h + 1, dirs, E, vcols)
                    lin_out(m, h, dirs, E, vcols, s0)
                osq = kt(m["osq"] if E == 2 else m["tA"], 4 * E)
                pe.wait_ge(sems["o_bank0"], e.more("o_bank0", 2))
                pe.wait_ge(sems["o_bank1"], e.more("o_bank1", 2))
                for pair in range(2):
                    for hh in range(2):
                        h = 2 * pair + hh
                        for x in range(E):
                            last = mm(BK[pair][:, hh * T:(hh + 1) * T], ones, osq[:, h * E + x, :],
                                      start=(x == 0), stop=(x == E - 1))
                last.then_inc(sems["oms"], 1)

            def rows_out(at_peer):
                pe.wait_ge(sems["y_out"], e.more("y_out"))
                y = (yN if at_peer else M2["yN"].rearrange("p (a d) -> p a d", a=2))
                for k in range(KT):
                    turn([y[:, tt, k * P:(k + 1) * P] for tt in range(2)])

            def peer(l):
                norm(hT)
                pe.wait_ge(sems["h"], e.more("h"))
                proj_cols(8, lambda k: hT[:, k, :], T)
                pe.wait_ge(sems["sub_in"], e.more("sub_in", 16))
                pe.wait_ge(*e.tile_out())
                qT = M5["qT"].rearrange("p (s t) -> p s t", s=16)
                for tt in range(2):
                    for h in range(PH):
                        bank = ring_bank()
                        for half in range(2):
                            last = mm(bank[:, half * P:(half + 1) * P], qT[:, 2 * h + half, tt * P:(tt + 1) * P],
                                      subT[:, half, :], start=True, stop=True)
                        last.then_inc(sems["turn"], 1)
                    pe.wait_ge(sems["routes"], e.more("routes"))
                    sel = M5["sel"].rearrange("p (b r n) -> p b r n", b=2, r=3)
                    bank = ring_bank()
                    for r in range(3):
                        last = pe.transpose(bank[:, r * P:(r + 1) * P], sel[:, tt, r, :], ident)
                    last.then_inc(sems["turn"], 1)
                def gates(first):
                    for b in range(2):
                        pe.wait_ge(sems["p2"], e.more("p2"))
                        if e.refill(f"g_bank{b}"):
                            pe.wait_ge(sems[f"g_bank{b}"], e.freed(f"g_bank{b}"))
                        for j in range(4):
                            last = mm(BK[6 + b][:, j * P:(j + 1) * P], P2[:, b, j, :], P1[:, b, j, :],
                                      start=True, stop=True)
                        last.then_inc(sems["g_mm"], 1)
                gates(True)
                with pe.Fori(0, 31) as i:
                    e.loop(i, {"p2": 2, "g_bank0": 1, "g_bank1": 1})
                    gates(False)
                    e.end_loop(31)

                def experts(first, last_one):
                    for pair in range(RING // 2):
                        u = next_panel().rearrange("p (k c) -> p k c", k=KT)
                        for j in range(2):
                            bank = ring_bank()
                            for k in range(KT):
                                last = mm(bank[:, 0:T], u[:, k, j * P:(j + 1) * P], hT[:, k, :], start=(k == 0), stop=(k == KT - 1))
                            last.then_inc(sems["proj"], 1)
                        v = next_panel().rearrange("p (j d) -> p j d", j=2)
                        for j in range(2):
                            pe.wait_ge(sems["w_ready"], e.more("w_ready"))
                            start = first and pair == 0 and j == 0
                            stop = last_one and pair == RING // 2 - 1 and j == 1
                            for tt in range(2):
                                for hf in range(2):
                                    last = mm(BK[2 * tt + hf][:, :], w_t[:, j, tt * P:(tt + 1) * P], v[:, j, hf * 512:(hf + 1) * 512],
                                              start=start, stop=stop)
                            if j == 1:
                                last.then_inc(sems["rows"], 1)
                            else:
                                last.then_inc(sems["w_free0"], 1)
                times = 64 // (RING // 2)
                experts(True, False)
                with pe.Fori(0, times - 2) as i:
                    e.loop(i, {**{f"loaded{n}": 16 for n in range(RING)}, "bank4": RING // 2, "bank5": RING // 2,
                               "w_ready": RING})
                    experts(False, False)
                    e.end_loop(times - 2)
                experts(False, True)
                e.tile += RING * (times - 3)
                panel[0] += RING * (times - 3)
                rows_out(True)

            pe.wait_ge(sems["consts_in"], e.more("consts_in", 48))
            mod_stage(24, ctx_panels=8)
            norm(Hc)
            norm(Hx)
            pe.wait_ge(sems["h"], e.more("h", 2))
            proj_cols(4, lambda k: H[:, k, :], 2 * T)
            proj_rows(2, lambda k, tt: H[:, k, tt * P:(tt + 1) * P], 4)
            proj_cols(6, lambda k: Hx[:, k, :], T)
            proj_rows(2, lambda k, tt: Hx[:, k, tt * P:(tt + 1) * P], 2)
            proj_cols(8, lambda k: Hx[:, k, :], T)
            vN1 = M1["vN"].rearrange("p (t n) -> p t n", t=4)
            for d in range(2):
                pe.wait_ge(sems["wctx"], e.more("wctx"))
                for h in range(HEADS):
                    w = kt(W_[d], 4)
                    turn([w[:, h, 0:P], w[:, h, P:2 * P]])
                    pe.wait_ge(*e.tile_out())
                    if e.refill("s0_in"):
                        pe.wait_ge(sems["s0_in"], e.freed("s0_in"))
                    kb = M1["kN"][:, 0:256].rearrange("p (t n) -> p t n", t=2)
                    for tt in range(2):
                        last = mm(BK[6][:, 0:P], kb[:, tt, :], vN1[:, tt, h * P:(h + 1) * P], start=(tt == 0), stop=(tt == 1))
                    last.then_inc(sems["s0"], 1)
            pe.wait_ge(sems["s0_in"], e.more("s0_in", 8))
            S0 = M1["S0"].rearrange("p (d h n) -> p d h n", d=2, h=4)
            lin(M1, 2, 1, lambda tt, h: vN1[:, 2 + tt, h * P:(h + 1) * P], lambda d, h: S0[:, d, h, :])
            pe.wait_ge(sems["vln"], e.more("vln", 1))
            pe.wait_ge(sems["x_in"], e.more("x_in", 64))
            vS = M1["vS"].rearrange("p (t n) -> p t n", t=2)
            for g in range(4):
                bank = ring_bank()
                for tt in range(2):
                    last = mm(bank[:, tt * P:(tt + 1) * P], vS[:, tt, g * P:(g + 1) * P], wsT[:, g, :], start=True, stop=True)
                last.then_inc(sems["turn"], 1)
            pe.wait_ge(sems["o_done"], e.more("o_done"))
            oT = kt(M1["oT"], 4)
            u4 = kt(M1["u"], 4)
            proj_cols(2, lambda k: oT[:, k, :], T, ks=4, tiles=4)
            pe.wait_ge(sems["sgu"], e.more("sgu"))
            proj_cols(2, lambda k: u4[:, k, :], T, ks=4, tiles=4)
            pe.wait_ge(sems["merged"], e.more("merged"))
            mg = kt(M1["fg0"], 8)
            proj_cols(4, lambda k: mg[:, k, :], T)
            norm(hT)
            pe.wait_ge(sems["h"], e.more("h"))
            proj_cols(22, lambda k: hT[:, k, :], T)
            pe.wait_ge(*e.tile_out())
            hf = kt(M2["hf"], FT)
            for n in range(FT // 2):
                w = next_panel().rearrange("p (j d) -> p j d", j=2)
                for j in range(2):
                    for tt in range(2):
                        for x in range(2):
                            last = mm(BK[2 * tt + x][:, :], hf[:, 2 * n + j, tt * P:(tt + 1) * P], w[:, j, x * 512:(x + 1) * 512],
                                      start=(n == 0 and j == 0), stop=(n == FT // 2 - 1 and j == 1))
                last.then_inc(sems["rows"], 1)
            rows_out(False)
            norm(hT)
            e.skip("h", 1)
            mod_stage(24)
            norm(hT)
            pe.wait_ge(sems["h"], e.more("h"))
            pe.wait_ge(sems["wgl_in"], e.more("wgl_in", 16))
            bank = ring_bank()
            for k in range(KT):
                last = mm(bank[0:16, 0:T], wgl[:, k, :], hT[:, k, :], start=(k == 0), stop=(k == KT - 1))
            last.then_inc(sems["turn"], 1)
            pe.wait_ge(sems["wg2_in"], e.more("wg2_in", 16))
            pe.wait_ge(*e.tile_out())
            for h in range(HEADS):
                bank = ring_bank()
                mm(bank[:, 0:T], M3["wg2"][0:16, h * P:(h + 1) * P], M3["glT"][0:16, :], start=True, stop=True).then_inc(sems["turn"], 1)
            proj_cols(4, lambda k: hT[:, k, :], T)
            proj_rows(4, lambda k, tt: hT[:, k, tt * P:(tt + 1) * P], 2)
            proj_cols(4, lambda k: hT[:, k, :], T)
            vN3 = M3["vN"].rearrange("p (t n) -> p t n", t=2)
            lin(M3, 1, 2, lambda tt, h: vN3[:, tt, h * 2 * P:(h + 1) * 2 * P], None)
            pe.wait_ge(sems["o_done"], e.more("o_done"))
            o8 = kt(M3["oT"], 8)
            proj_cols(4, lambda k: o8[:, k, :], T)
            peer(0)
            mod_stage(8)
            norm(hT)
            pe.wait_ge(sems["h"], e.more("h"))
            proj_cols(2, lambda k: hT[:, k, :], T)
            proj_rows(1, lambda k, tt: hT[:, k, tt * P:(tt + 1) * P], 2)
            mod_stage(24)
            norm(hT)
            pe.wait_ge(sems["h"], e.more("h"))
            proj_cols(4, lambda k: hT[:, k, :], T)
            kS, qS = kt(M4["kS"], 4), kt(M4["qS"], 8)
            pe.wait_ge(*e.tile_out())
            for n in range(12):
                src = kS[:, n, :] if n < 4 else qS[:, n - 4, :]
                bank = ring_bank()
                mm(bank[:, 0:T], C("rot"), src, start=True, stop=True).then_inc(sems["turn"], 1)
            pe.wait_ge(sems["roped"], e.more("roped", 1))
            pS = M4["pS"].rearrange("p (b n) -> p b n", b=2)
            pT = M4["pT"].rearrange("p (b n) -> p b n", b=2)
            vP = M4["vP"].rearrange("p (t g s n) -> p t g s n", t=2, g=4, s=2)
            pe.wait_ge(sems["vpad"], e.more("vpad"))

            def att_scores(h):
                g, r = h // 4, slice(64 * (h % 2), 64 * (h % 2) + 64)
                b = BK[h % 2]
                q = qS[r, h // 2, :]
                if h >= 2:
                    pe.wait_ge(sems["att_sfree"], e.more("att_sfree"))
                mm(b[:, 0:P], q[:, 0:P], kS[r, g, 0:P], start=True, stop=True)
                mm(b[:, P:3 * P], q[:, P:2 * P], kS[r, g, 0:2 * P], start=True, stop=True).then_inc(sems["att_s"], 1)

            def att_out(h):
                pe.wait_ge(*e.tile_out())
                g, s, j = h // 4, h % 2, h // 2
                b = BK[2 + j % 2]
                if s == 0:
                    if e.refill(f"att_bank{j % 2}"):
                        pe.wait_ge(sems[f"att_bank{j % 2}"], e.freed(f"att_bank{j % 2}"))
                mm(b[:, 0:P], vP[:, 0, g, s, :], pT[:, h % 2, 0:P], start=(s == 0), stop=False, skip_group_check=True)
                mm(b[:, P:2 * P], vP[:, 0, g, s, :], pT[:, h % 2, P:2 * P], start=False, stop=False, skip_group_check=True)
                last = mm(b[:, P:2 * P], vP[:, 1, g, s, :], pT[:, h % 2, 2 * P:3 * P], start=False, stop=(s == 1), skip_group_check=True)
                last.then_inc(sems["att_o"], 1)

            att_scores(0)
            att_scores(1)
            for h in range(16):
                pe.wait_ge(sems["att_p"], e.more("att_p"))
                turn([pS[:, h % 2, n * P:(n + 1) * P] for n in range(3)])
                if h + 2 < 16:
                    att_scores(h + 2)
                att_out(h)
            pe.wait_ge(sems["att_bank0"], e.more("att_bank0", 4))
            pe.wait_ge(sems["att_bank1"], e.more("att_bank1", 4))
            oS = kt(M4["oS"], 8)
            proj_cols(4, lambda k: oS[:, k, :], T)
            peer(1)
            norm(hT)
            pe.wait_ge(sems["h"], e.more("h"))
            for tt in range(2):
                for x in range(2):
                    bank = ring_bank()
                    for j in range(4):
                        last = pe.transpose(bank[:, j * P:(j + 1) * P], xT[:, 4 * x + j, tt * P:(tt + 1) * P], ident)
                    last.then_inc(sems["turn"], 1)

        @block.scalar
        def _(act):
            e = Counts(sems)
            A = act.activation

            def evac(name, dst, func, width=T, split=None, **kw):
                b = 4 + e.tile % 2
                e.tile += 1
                act.wait_ge(sems[name], e.more(name))
                src = BK[b][:, 0:width]
                if split:
                    src = src.rearrange("p (t n) -> p t n", t=split)
                A(dst, src, func, **kw).then_inc(sems[f"bank{b}"], 1)

            def norm(src, dst, shift):
                for k in range(KT):
                    A(dst[:, k, :], src[:, k, :], ACT.Square).then_inc(sems["sq"], 1)
                act.wait_ge(sems["var"], e.more("var"))
                A(nrm[:, 1, :], nrm[:, 0, :], ACT.Sqrt).then_inc(sems["std"], 1)
                if shift is not None:
                    for k in range(KT):
                        act.wait_ge(sems["hs"], e.more("hs"))
                        last = A(dst[:, k, :], dst[:, k, :], ACT.Identity, bias=modc[:, shift + k:shift + k + 1])
                    last.then_inc(sems["h"], 1)

            def residual(name):
                e.tiles(name, 8)
                act.wait_ge(*e.tile_out())

            def rows_out(n, y):
                act.wait_ge(sems["rows"], e.more("rows", n))
                for tt in range(2):
                    for x in range(2):
                        last = A(y[:, tt, x * 512:(x + 1) * 512], BK[2 * tt + x][:, :], ACT.Copy)
                last.then_inc(sems["y_out"], 1)

            def lin(m, dirs, E, root_buf):
                oT, osq = kt(m["oT"], 4 * E), kt(m["osq"] if E == 2 else m["tA"], 4 * E)

                def turned(h):
                    for d in range(dirs):
                        evac("turn", kview(m, h, d, dirs), ACT.Copy, split=2)
                turned(0)
                for h in range(HEADS):
                    if h + 1 < HEADS:
                        turned(h + 1)
                    act.wait_ge(sems["o_sum"], e.more("o_sum"))
                    src = BK[2 + h % 2][:, 0:E * T].rearrange("p (x t) -> p x t", x=E)
                    A(oT[:, h * E:(h + 1) * E, :], src, ACT.Copy)
                    A(osq[:, h * E:(h + 1) * E, :], src, ACT.Square).then_inc(sems[f"o_bank{h % 2}"], 1)
                act.wait_ge(sems["ovar"], e.more("ovar"))
                A(root_buf, root_buf, ACT.Sqrt).then_inc(sems["ostd"], 1)

            def peer(l, scale_col, shift):
                norm(xT, hT, shift)
                qT = M5["qT"].rearrange("p (s t) -> p s t", s=16)
                for s in range(16):
                    evac("proj", qT[:, s, :], ACT.Copy)
                for tt in range(2):
                    e.tiles("turn", 8)
                    act.wait_ge(sems["peer_sm"], e.more("peer_sm"))
                    A(M5["cv"][:, 0:128], M5["cv"][:, 0:128], ACT.Exp).then_inc(sems["peer_ex"], 1)
                    evac("turn", routes[:, :, tt * P:(tt + 1) * P], ACT.Copy, width=3 * P, split=3)

                def gates(at):
                    for b in range(2):
                        act.wait_ge(sems["g_mm"], e.more("g_mm"))
                        A(G[:, :, bass.ds(at + 4 * b, 4)].rearrange("p i t -> p t i"),
                          BK[6 + b][:, :].rearrange("p (t i) -> p t i", t=4), ACT.Copy).then_inc(sems[f"g_bank{b}"], 1)
                gates(0)
                with act.Fori(0, 31) as i:
                    e.loop(i, {"g_mm": 2})
                    gates(i * 8 + 8)
                    e.end_loop(31)

                def experts(first):
                    for pair in range(RING // 2):
                        for j in range(2):
                            b = 4 + e.tile % 2
                            e.tile += 1
                            act.wait_ge(sems["proj"], e.more("proj"))
                            if first and pair == 0:
                                pass
                            else:
                                act.wait_ge(sems["w_ready"], e.value("w_ready", w0[0] - 1))
                            w0[0] += 1
                            A(gelu_t[:, j, :], BK[b][:, 0:T], ACT.Gelu).then_inc(sems[f"bank{b}"], 1)
                w0 = [l * P]
                experts(True)
                times = 64 // (RING // 2)
                with act.Fori(0, times - 1) as i:
                    e.loop(i, {"proj": RING, "w_ready": RING})
                    experts(False)
                    e.end_loop(times - 1)
                e.tile += RING * (times - 2)
                rows_out(64, yN)
                residual("turn")

            act.wait_ge(sems["consts_in"], e.more("consts_in", 48))
            A(cact[:, 0:24], vec[:, 0:24], ACT.Silu).then_inc(sems["cact"], 1)
            act.wait_ge(sems["lb"], e.more("lb"))
            A(lbs[:, 0, :], lbs[:, 0, :], ACT.Sigmoid).then_inc(sems["gate"], 1)
            act.wait_ge(sems["x_in"], e.more("x_in", 64))
            norm(ctxT, Hc, 48)
            norm(xT, Hx, 0)
            for d in range(2):
                for h in range(4):
                    evac("proj", fg[d][:, h, :], ACT.Sigmoid, width=2 * T)
            vN1 = M1["vN"].rearrange("p (t n) -> p t n", t=4)
            for c in range(2):
                for tt in range(4):
                    evac("proj", vN1[:, tt, c * 2 * P:(c + 1) * 2 * P], ACT.Copy)
            for d in range(2):
                act.wait_ge(sems["gates_f"], e.more("gates_f"))
                A(cum[d], fg[d], ACT.Ln).then_inc(sems["logf"], 1)
            for h in range(4):
                evac("proj", kt(M1["q"], 4)[:, h, :], ACT.Copy)
            for h in range(4):
                evac("proj", kt(M1["og"], 4)[:, h, :], ACT.Silu)
            for h in range(4):
                evac("proj", kt(M1["u"], 4)[:, h, :], ACT.Gelu_apprx_tanh)
            vS1 = M1["vS"].rearrange("p (t n) -> p t n", t=2)
            for c in range(2):
                for tt in range(2):
                    evac("proj", vS1[:, tt, c * 2 * P:(c + 1) * 2 * P], ACT.Gelu_apprx_tanh)
            for k in range(KT):
                evac("proj", ctxT[:, k, :], ACT.Sigmoid)
            for k in range(KT):
                evac("proj", Hc[:, k, :], ACT.Sigmoid)
            act.wait_ge(sems["vvar"], e.more("vvar"))
            A(M1["stat"][:, 12:14], M1["stat"][:, 12:14], ACT.Sqrt).then_inc(sems["vstd"], 1)
            for d in range(2):
                act.wait_ge(sems["cums"], e.more("cums"))
                at = T - 1 if d == 0 else 0
                for h in range(4):
                    last = A(kt(W_[d], 4)[:, h, :], cum[d][:, h, 0:T], ACT.Exp, scale=-1.0, bias=cum[d][:, h, at:at + 1])
                last.then_inc(sems["wexp"], 1)
            for n in range(8):
                evac("turn", M1["kN"][:, 0:T], ACT.Copy)
            for d in range(2):
                act.wait_ge(sems["expo"], e.more("expo"))
                x4, t0 = xpart(M1[f"cum{d}"]), CHUNK - 1 if d == 0 else 0
                A(M1[f"qi{d}"], M1["tA"], ACT.Exp)
                A(M1[f"ki{d}"], M1["tA"], ACT.Exp, scale=-1.0)
                A(M1[f"kd{d}"], M1["tB"], ACT.Exp)
                A(chunks(M1[f"qd{d}"]), x4, ACT.Exp)
                A(M1["dec"][:, d * 16:(d + 1) * 16].rearrange("p (h c) -> p h c", h=4), x4[:, :, :, t0], ACT.Exp
                  ).then_inc(sems["exps"], 1)
            lin(M1, 2, 1, M1["tB"])
            e.tiles("turn", 4)
            e.tiles("proj", 16)
            residual("proj")
            norm(xT, hT, 24)
            sil = M2["sil"].rearrange("p (b j t) -> p b j t", b=2, j=2)
            for n in range(FT // 2):
                if n >= 2:
                    act.wait_ge(*e.tile_out(5))
                for j in range(2):
                    evac("proj", sil[:, n % 2, j, :], ACT.Silu)
                e.tiles("proj", 2)
            rows_out(FT // 2, M2["yN"].rearrange("p (a d) -> p a d", a=2))
            residual("turn")
            norm(xT, hT, None)
            act.wait_ge(sems["h"], 4)
            norm(xT, hT, 0)
            evac_gl = 4 + e.tile % 2
            e.tile += 1
            act.wait_ge(sems["turn"], e.more("turn"))
            A(M3["glT"][0:16, :], BK[evac_gl][0:16, 0:T], ACT.Copy).then_inc(sems[f"bank{evac_gl}"], 1)
            zA, zB = kt(M3["zA"], 4), kt(M3["zB"], 4)
            b0 = VEC["gla_b_g2"][0]
            for h in range(4):
                evac("turn", zA[:, h, :], ACT.Identity, bias=vec[:, b0 + h:b0 + h + 1])
            act.wait_ge(*e.tile_out())
            A(M3["zB"], M3["zA"], ACT.Abs).then_inc(sems["act_step"], 1)
            act.wait_ge(sems["act_step"], e.stepped())
            A(M3["zB"], M3["zB"], ACT.Exp, scale=-1.0).then_inc(sems["act_step"], 1)
            act.wait_ge(sems["act_step"], e.stepped())
            A(M3["zB"], M3["zB"], ACT.Ln, bias=ones[:, 0:1]).then_inc(sems["zln"], 1)
            for h in range(4):
                evac("proj", kt(M3["q"], 4)[:, h, :], ACT.Copy, scale=float(P) ** -0.5)
            for h in range(4):
                evac("proj", kt(M3["k"], 4)[:, h, :], ACT.Copy)
            vN3 = M3["vN"].rearrange("p (t n) -> p t n", t=2)
            for c in range(4):
                for tt in range(2):
                    evac("proj", vN3[:, tt, c * 2 * P:(c + 1) * 2 * P], ACT.Copy)
            for h in range(8):
                evac("proj", kt(M3["og"], 8)[:, h, :], ACT.Silu)
            act.wait_ge(sems["expo"], e.more("expo"))
            tau = 1.0 / 16.0
            A(M3["qi0"], M3["cum0"], ACT.Exp, scale=tau)
            A(M3["ki0"], M3["cum0"], ACT.Exp, scale=-tau)
            A(M3["kd0"], M3["tA"], ACT.Exp, scale=tau)
            A(M3["dec"][:, 0:16].rearrange("p (h c) -> p h c", h=4), chunks(M3["cum0"])[:, :, :, CHUNK - 1], ACT.Exp,
              scale=tau).then_inc(sems["exps"], 1)
            lin(M3, 1, 2, M3["zA"])
            residual("proj")
            peer(0, 32, 24)
            norm(xT, hT, 0)
            for g in range(4):
                evac("proj", kt(M4["kS"], 4)[:, g, :], ACT.Copy)
            for tt in range(2):
                evac("proj", M4["vS"].rearrange("p (t n) -> p t n", t=2)[:, tt, :], ACT.Copy)
            act.wait_ge(sems["trig"], e.more("trig"))
            A(M4["sinT"], M4["ang"][:, 0:T], ACT.Sin)
            A(M4["cosT"], M4["ang"][:, T:2 * T], ACT.Sin, scale=-1.0, bias=C("half_pi")).then_inc(sems["rope_in"], 1)
            norm(xT, hT, 0)
            for j in range(8):
                evac("proj", kt(M4["qS"], 8)[:, j, :], ACT.Copy)
            e.tiles("turn", 12)
            sS = M4["sS"].rearrange("p (b n) -> p b n", b=2)
            pS = M4["pS"].rearrange("p (b n) -> p b n", b=2)
            pT = M4["pT"].rearrange("p (b n) -> p b n", b=2)
            am = M4["am"].rearrange("p (b n) -> p b n", b=2)

            def att_exp(h):
                b = h % 2
                act.wait_ge(sems["att_max"], e.more("att_max"))
                A(pS[:, b, 0:P], sS[:, b, 0:P], ACT.Exp, bias=am[:, b, 2:3], accum_out=am[:, b, 6:7])
                A(pS[:, b, P:3 * P], sS[:, b, P:3 * P], ACT.Exp, bias=am[:, b, 3:4], accum_out=am[:, b, 7:8])
                A(am[:, b, 4:6], am[:, b, 4:6], ACT.Exp).then_inc(sems["att_exp"], 1)

            att_exp(0)
            for h in range(16):
                if h + 1 < 16:
                    att_exp(h + 1)
                evac("turn", pT[:, h % 2, :], ACT.Copy, width=3 * P)
                act.wait_ge(sems["att_o"], e.more("att_o"))
                if h % 2:
                    j = h // 2
                    A(kt(M4["oS"], 8)[:, j, :], BK[2 + j % 2][:, 0:T], ACT.Copy).then_inc(sems[f"att_bank{j % 2}"], 1)
            residual("proj")
            peer(1, 32, 24)
            norm(xT, hT, None)
            y = H[:, :, :].rearrange("p k t -> p (k t)")[:, 0:2048].rearrange("p (a d) -> p a d", a=2)
            for tt in range(2):
                for x in range(2):
                    evac("turn", y[:, tt, x * 512:(x + 1) * 512], ACT.Copy, width=512)
            act.wait_ge(*e.tile_out())
            act.dma_start(out.rearrange("o (a p) d -> p (o a) d", p=P), y).then_inc(sems["out_done"], 16)
            act.wait_ge(sems["out_done"], 16)

        @block.vector
        def _(dve):
            e = Counts(sems)
            TT, TS, STT = dve.tensor_tensor, dve.tensor_scalar, dve.scalar_tensor_tensor

            def ring_tile(name):
                b = 4 + e.tile % 2
                e.tile += 1
                dve.wait_ge(sems[name], e.more(name))
                return BK[b], sems[f"bank{b}"]

            panel = [0]
            mods = [0]

            def mod_stage(panels, c_col, bias, ctx_panels=0):
                def body(with_ctx, skip_first=False):
                    for r in range(RING):
                        dve.wait_ge(sems[f"loaded{(panel[0] + r) % RING}"], e.more(f"loaded{(panel[0] + r) % RING}", 16))
                        w = slot(panel[0] + r).rearrange("p (k c) -> p k c", k=KT)
                        if not (skip_first and r < 2):
                            dve.wait_ge(sems["mod_turn"], e.value("mod_turn", mods[0] - (0 if with_ctx else 1)))
                        elif with_ctx and r:
                            dve.wait_ge(sems["mod_turn"], mods[0])
                        mods[0] += 1
                        for which in ([1, 0] if with_ctx else [0]):
                            acc = macc[:, 2 if which else r % 2, :]
                            col = 8 if which else c_col
                            TS(acc, w[:, 0, :], cact[:, col:col + 1], None, MUL).then_inc(sems["dve_step"], 1)
                            dve.wait_ge(sems["dve_step"], e.stepped())
                            for k in range(1, KT):
                                ins = STT(acc, w[:, k, :], cact[:, col + k:col + k + 1], acc, MUL, ADD)
                                if which or k < KT - 1:
                                    ins.then_inc(sems["dve_step"], 1)
                                    dve.wait_ge(sems["dve_step"], e.stepped())
                        ins.then_inc(sems["mod_acc"], 1)
                for n in range(0, ctx_panels, RING):
                    body(True, n == 0 and mods[0] == 0)
                times = (panels - ctx_panels) // RING
                with dve.Fori(0, times) as i:
                    e.loop(i, {"dve_step": RING * (KT - 1), "mod_turn": RING, **{f"loaded{r}": 16 for r in range(RING)}})
                    body(False)
                    e.end_loop(times)
                mods[0] += RING * (times - 1)
                panel[0] += panels
                dve.wait_ge(sems["mod_turn"], mods[0])
                cols = 2 * panels
                ins = TT(modc[:, 0:cols], BK[6][:, 0:cols], bias, ADD)
                if ctx_panels:
                    ins = TT(modc[:, 48:64], BK[6][:, 48:64], bias[:, 0:16], ADD)
                ins.then_inc(sems["mod_bank"], 1)
                dve.wait_ge(sems["mod_bank"], mod_uses[0] + 1)
                mod_uses[0] += 1

            mod_uses = [0]

            def used(n):
                for _ in range(n):
                    e.skip(f"loaded{panel[0] % RING}", 16)
                    panel[0] += 1

            def make_gain(i, scale, g):
                STT(gain[:, i, :], modc[:, scale:scale + 8], 1.0, g, ADD, MUL).then_inc(sems["dve_step"], 1)
                dve.wait_ge(sems["dve_step"], e.stepped())

            def norm(src, dst, g, shift):
                dve.wait_ge(sems["ms"], e.more("ms"))
                TS(nrm[:, 0, :], BK[7][:, 0:T], 1.0 / D, EPS, MUL, ADD).then_inc(sems["var"], 1)
                dve.wait_ge(sems["std"], e.more("std"))
                dve.reciprocal(nrm[:, 0, :], nrm[:, 1, :]).then_inc(sems["dve_step"], 1)
                dve.wait_ge(sems["dve_step"], e.stepped())
                for k in range(KT):
                    ins = STT(dst[:, k, :], src[:, k, :], g[:, k:k + 1], nrm[:, 0, :], MUL, MUL)
                    if shift:
                        ins.then_inc(sems["hs"], 1)
                if not shift:
                    ins.then_inc(sems["h"], 1)

            def residual(name, gate):
                for k in range(KT):
                    bank, free = ring_tile(name)
                    STT(xT[:, k, :], bank[:, 0:T], modc[:, gate + k:gate + k + 1], xT[:, k, :], MUL, ADD).then_inc(free, 1)
                dve.wait_ge(*e.tile_out())

            lins = [0, 0]

            def lin(m, dirs, E, g, root_buf, dv, s0):
                sc = m["sc"].rearrange("p (b q n) -> p b q n", b=2, q=4)
                oT = kt(m["oT"], 4 * E)
                for h in range(HEADS):
                    dve.wait_ge(sems["scores"], e.more("scores"))
                    if h >= 2:
                        dve.wait_ge(sems["o_sum"], lins[0] + h - 1)
                    for d in range(dirs):
                        for hf in range(2):
                            rows, cols = slice(64 * hf, 64 * hf + 64), slice(64 * hf, 64 * hf + 64)
                            src = BK[h % 2][:, :].rearrange("p (q n) -> p q n", q=4)
                            ins = dve.copy_predicated(sc[rows, h % 2, 2 * d:2 * d + 2, cols],
                                                      masks[rows, d, :, :], src[rows, 2 * d:2 * d + 2, cols])
                    ins.then_inc(sems["masked"], 1)
                    for d in range(dirs):
                        dve.wait_ge(sems["dstate"], e.more("dstate"))
                        for r in range(3):
                            c = r if d == 0 else NCH - 1 - r
                            dec = m["dec"][:, d * 16 + h * 4 + c:d * 16 + h * 4 + c + 1]
                            b, col = BK[6 + c % 2], c // 2 * E * P
                            before = s0(d, h) if r == 0 else state(m, h, d, r - 1, dirs, E)
                            if before is None:
                                ins = dve.tensor_copy(state(m, h, d, r, dirs, E), b[:, col:col + E * P])
                            else:
                                ins = STT(state(m, h, d, r, dirs, E), before, dec, b[:, col:col + E * P], MUL, ADD)
                            if r < 2:
                                ins.then_inc(sems["dve_step"], 1)
                                dve.wait_ge(sems["dve_step"], e.stepped())
                        ins.then_inc(sems["state"], 1)
                lins[0] += HEADS
                dve.wait_ge(sems["oms"], e.more("oms"))
                for pair in range(2):
                    ins = TS(root_buf[:, pair * 512:(pair + 1) * 512], BK[pair][:, :], 1.0 / dv, EPS, MUL, ADD)
                ins.then_inc(sems["ovar"], 1)
                dve.wait_ge(sems["ostd"], e.more("ostd"))
                dve.reciprocal(root_buf, root_buf).then_inc(sems["dve_step"], 1)
                dve.wait_ge(sems["dve_step"], e.stepped())
                for h in range(HEADS):
                    for x in range(E):
                        ins = STT(oT[:, h * E + x, :], oT[:, h * E + x, :], g[:, x:x + 1], root_buf[:, h * T:(h + 1) * T], MUL, MUL)
                ins.then_inc(sems["dve_step"], 1)
                dve.wait_ge(sems["dve_step"], e.stepped())
                TT(m["oT"], m["oT"], m["og"], MUL).then_inc(sems["o_done"], 1)

            iota16 = iota[:, 0:16].unsqueeze(1).broadcast_to([P, P, 16])

            def peer(l):
                make_gain(0, 32, V("norm_g_2")[:, (2 * l + 1) * 8:(2 * l + 2) * 8])
                norm(xT, hT, gain[:, 0, :], True)
                e.tiles("proj", 16)
                topv = M5["topv"][:, 0:256].rearrange("p (h s k) -> p h s k", h=8, s=2)
                topi = M5["topi"][:, 0:256].bitcast(u32).rearrange("p (h s k) -> p h s k", h=8, s=2)
                topif = M5["topif"][:, 0:256].rearrange("p (h s k) -> p h s k", h=8, s=2)
                s2, cand, cand2 = M5["s2"], M5["cand"], M5["cand2"]
                cv = M5["cv"][:, 0:128].rearrange("p (h k) -> p h k", h=8)
                ci = M5["ci"][:, 0:128].bitcast(u32).rearrange("p (h k) -> p h k", h=8)
                sel = M5["sel"].rearrange("p (b r n) -> p b r n", b=2, r=3)
                eq = M5["eq"].rearrange("p (n a) -> p n a", a=16)
                low = -3.0e38

                def top16(src, rest, values, indices, freed):
                    dve.max(values[:, 0:8], src).then_inc(sems["dve_step"], 1)
                    dve.wait_ge(sems["dve_step"], e.stepped())
                    dve.max_index(indices[:, 0:8], values[:, 0:8], src)
                    ins = dve.match_replace(rest, values[:, 0:8], src, low)
                    if freed is None:
                        ins.then_inc(sems["dve_step"], 1)
                        dve.wait_ge(sems["dve_step"], e.stepped())
                    else:
                        ins.then_inc(freed, 1)
                        dve.wait_ge(*e.tile_out())
                    dve.max(values[:, 8:16], rest).then_inc(sems["dve_step"], 1)
                    dve.wait_ge(sems["dve_step"], e.stepped())
                    dve.max_index(indices[:, 8:16], values[:, 8:16], rest).then_inc(sems["dve_step"], 1)
                    dve.wait_ge(sems["dve_step"], e.stepped())

                for tt in range(2):
                    for h in range(PH):
                        bank, free = ring_tile("turn")
                        for half in range(2):
                            top16(bank[:, half * P:(half + 1) * P], s2[:, 0:P], topv[:, h, half, :], topi[:, h, half, :],
                                  free if half else None)
                    dve.tensor_copy(M5["topif"][:, 0:256], M5["topi"][:, 0:256].bitcast(u32))
                    for h in range(PH):
                        TT(cand.rearrange("p (a b) -> p a b", a=16), topv[:, h, 0, :].unsqueeze(2).broadcast_to([P, 16, 16]),
                                  topv[:, h, 1, :].unsqueeze(1).broadcast_to([P, 16, 16]), ADD).then_inc(sems["dve_step"], 1)
                        dve.wait_ge(sems["dve_step"], e.stepped())
                        top16(cand, cand2, cv[:, h, :], ci[:, h, :], None)
                    TT(M5["sm"][:, 0:8], cv[:, :, 0], cv[:, :, 0], ALU.max).then_inc(sems["dve_step"], 1)
                    dve.wait_ge(sems["dve_step"], e.stepped())
                    TT(cv, cv, M5["sm"][:, 0:8].unsqueeze(2).broadcast_to([P, 8, 16]), SUB).then_inc(sems["peer_sm"], 1)
                    cu = M5["ci"][:, 0:128].bitcast(u32)
                    TS(M5["ca"][:, 0:128].bitcast(u32), cu, 4, None, ALU.logical_shift_right)
                    TS(M5["cb"][:, 0:128].bitcast(u32), cu, 15, None, ALU.bitwise_and).then_inc(sems["dve_step"], 1)
                    dve.wait_ge(sems["dve_step"], e.stepped())
                    dve.tensor_copy(M5["caf"][:, 0:128], M5["ca"][:, 0:128].bitcast(u32))
                    dve.tensor_copy(M5["cbf"][:, 0:128], M5["cb"][:, 0:128].bitcast(u32)).then_inc(sems["dve_step"], 1)
                    dve.wait_ge(sems["dve_step"], e.stepped())
                    for half, place in enumerate(("caf", "cbf")):
                        TT(eq, M5[place][:, 0:128].unsqueeze(2).broadcast_to([P, P, 16]), iota16, ALU.is_equal).then_inc(sems["dve_step"], 1)
                        dve.wait_ge(sems["dve_step"], e.stepped())
                        e4 = M5["eq"].rearrange("p (h k a) -> p h k a", h=8, k=16)
                        TT(e4, e4, topif[:, :, half, :].unsqueeze(2).broadcast_to([P, 8, 16, 16]), MUL).then_inc(sems["dve_step"], 1)
                        dve.wait_ge(sems["dve_step"], e.stepped())
                        dve.tensor_reduce(sel[:, tt, half, :], eq, AX.X, ADD).then_inc(sems["dve_step"], 1)
                        dve.wait_ge(sems["dve_step"], e.stepped())
                    dve.wait_ge(sems["peer_ex"], e.more("peer_ex"))
                    dve.tensor_reduce(M5["sm"][:, 8:16], cv, AX.X, ADD).then_inc(sems["dve_step"], 1)
                    dve.wait_ge(sems["dve_step"], e.stepped())
                    dve.reciprocal(M5["sm"][:, 16:24], M5["sm"][:, 8:16]).then_inc(sems["dve_step"], 1)
                    dve.wait_ge(sems["dve_step"], e.stepped())
                    TT(sel[:, tt, 2, :].rearrange("p (h k) -> p h k", h=8), cv,
                       M5["sm"][:, 16:24].unsqueeze(2).broadcast_to([P, 8, 16]), MUL).then_inc(sems["routes"], 1)
                    e.tiles("turn", 1)
                dve.wait_ge(*e.tile_out())

                def onehots(first, at):
                    for b in range(2):
                        if not first:
                            dve.wait_ge(sems["g_mm"], e.value("g_mm", 64 * l + 1 + b))
                        for j in range(4):
                            t = at + 4 * b + j
                            TS(P2[:, b, j, :], iota, routes[:, 1, bass.ds(t, 1)], routes[:, 2, bass.ds(t, 1)], ALU.is_equal, MUL)
                            ins = TS(P1[:, b, j, :], iota, routes[:, 0, bass.ds(t, 1)], None, ALU.is_equal)
                        ins.then_inc(sems["p2"], 1)
                onehots(True, 0)
                with dve.Fori(0, 31) as i:
                    e.loop(i, {"g_mm": 2})
                    onehots(False, i * 8 + 8)
                    e.end_loop(31)
                dve.wait_ge(sems["g_bank0"], 32 * (l + 1))
                dve.wait_ge(sems["g_bank1"], 32 * (l + 1))

                def experts(first, at):
                    for pair in range(RING // 2):
                        for j in range(2):
                            e.tile += 1
                            dve.wait_ge(*e.tile_out())
                            if not (first and pair == 0):
                                name, base = ("w_free0", 64 * l) if j == 0 else ("rows", FT // 2 + 64 * l)
                                dve.wait_ge(sems[name], e.value(name, base + pair + (0 if first else RING // 2)))
                            TT(w_t[:, j, :], gelu_t[:, j, :], G[:, bass.ds(at + 2 * pair + j, 1), :].rearrange("p o t -> p (o t)"), MUL).then_inc(sems["w_ready"], 1)
                experts(True, 0)
                times = 64 // (RING // 2)
                with dve.Fori(0, times - 1) as i:
                    e.loop(i, {"bank4": RING // 2, "bank5": RING // 2, "w_free0": RING // 2, "rows": RING // 2})
                    experts(False, i * RING + RING)
                    e.end_loop(times - 1)
                e.tile += RING * (times - 2)
                e.skip("proj", 128)
                used(128 + 8)
                residual("turn", 40)

            dve.wait_ge(sems["consts_in"], e.more("consts_in", 48))
            g = V("lb_gamma").rearrange("p (l n) -> p l n", l=2)
            TT(lbs[:, 0, :], g[:, 0, :], g[:, 1, :], SUB).then_inc(sems["lb"], 1)
            dve.wait_ge(sems["gate"], e.more("gate"))
            TS(lbs[:, 1, :], lbs[:, 0, :], -1.0, 1.0, MUL, ADD).then_inc(sems["dve_step"], 1)
            dve.wait_ge(sems["dve_step"], e.stepped())
            dve.wait_ge(sems["cact"], e.more("cact"))
            dve.wait_ge(sems["x_in"], e.more("x_in", 64))
            mod_stage(24, 0, V("b_mod"), ctx_panels=8)
            make_gain(1, 56, V("g_mix"))
            make_gain(0, 8, V("g_mix"))
            norm(ctxT, Hc, gain[:, 1, :], True)
            norm(xT, Hx, gain[:, 0, :], True)
            used(4 + 2 + 6 + 2 + 8)
            for d in range(2):
                e.tiles("proj", 4)
                dve.wait_ge(*e.tile_out())
                for h in range(4):
                    n = d * 4 + h
                    ins = TS(fg[d][:, h, :], fg[d][:, h, :], lbs[:, 1, n:n + 1], lbs[:, 0, n:n + 1], MUL, ADD)
                ins.then_inc(sems["gates_f"], 1)
            for d in range(2):
                dve.wait_ge(sems["logf"], e.more("logf"))
                TS(fg[d], fg[d], -1.0, 1.0, MUL, ADD)
                for h in range(4):
                    if d == 0:
                        ins = dve.tensor_tensor_scan(cum[d][:, h, :], M1["scan_f"], cum[d][:, h, :], 0.0, MUL, ADD)
                    else:
                        ins = dve.tensor_tensor_scan(cum[d][:, h, ::-1], M1["scan_b"][:, ::-1], cum[d][:, h, ::-1], 0.0, MUL, ADD)
                ins.then_inc(sems["cums"], 1)
                dve.wait_ge(sems["cums"], d + 1)
            e.tiles("proj", 8 + 12 + 4)
            dve.wait_ge(*e.tile_out())
            vS1 = M1["vS"].rearrange("p (t n) -> p t n", t=2)
            stat = M1["stat"]
            for tt in range(2):
                dve.bn_stats(stat[:, 0:6], vS1[:, tt, :]).then_inc(sems["dve_step"], 1)
                dve.wait_ge(sems["dve_step"], e.stepped())
                dve.bn_aggr(stat[:, 6 + 2 * tt:8 + 2 * tt], stat[:, 0:6]).then_inc(sems["dve_step"], 1)
                dve.wait_ge(sems["dve_step"], e.stepped())
            TS(stat[:, 12:14], stat[:, 7:10:2], EPS, None, ADD).then_inc(sems["vvar"], 1)
            dve.wait_ge(sems["vstd"], e.more("vstd"))
            dve.reciprocal(stat[:, 14:16], stat[:, 12:14]).then_inc(sems["dve_step"], 1)
            dve.wait_ge(sems["dve_step"], e.stepped())
            for tt in range(2):
                TS(vS1[:, tt, :], vS1[:, tt, :], stat[:, 6 + 2 * tt:7 + 2 * tt], stat[:, 14 + tt:15 + tt], SUB, MUL).then_inc(sems["dve_step"], 1)
                dve.wait_ge(sems["dve_step"], e.stepped())
                TT(vS1[:, tt, :], vS1[:, tt, :], M1["ln_v_g"], MUL).then_inc(sems["dve_step"], 1)
                dve.wait_ge(sems["dve_step"], e.stepped())
                ins = TT(vS1[:, tt, :], vS1[:, tt, :], M1["ln_v_b"], ADD)
            ins.then_inc(sems["vln"], 1)
            for d in range(2):
                dve.wait_ge(sems["wexp"], e.more("wexp"))
                TT(kt(W_[d], 4), kt(W_[d], 4), fg[d][:, :, 0:T], MUL).then_inc(sems["wctx"], 1)
            e.tiles("proj", 16)
            S0 = M1["S0"].rearrange("p (d h n) -> p d h n", d=2, h=4)
            for n in range(8):
                dve.wait_ge(sems["s0"], e.more("s0"))
                dve.tensor_copy(S0[:, n // 4, n % 4, :], BK[6][:, 0:P]).then_inc(sems["s0_in"], 1)
            e.tiles("turn", 8)
            dve.memset(M1["sc"], 0.0).then_inc(sems["dve_step"], 1)
            dve.wait_ge(sems["dve_step"], e.stepped())
            for d in range(2):
                x4, t0 = xpart(M1[f"cum{d}"]), CHUNK - 1 if d == 0 else 0
                last = x4[:, :, :, t0:t0 + 1].broadcast_to([P, 4, NCH, CHUNK])
                for h in range(4):
                    STT(chunks(M1["tA"])[:, h], last[:, h], -0.5, x4[:, h], MUL, ADD)
                TT(chunks(M1["tB"]), last, x4, SUB).then_inc(sems["expo"], 1)
                dve.wait_ge(sems["exps"], e.more("exps"))
                k4 = xpart(M1[f"fg{d}"])
                TT(M1[f"qi{d}"], M1[f"qi{d}"], M1["q"], MUL)
                TT(M1[f"qd{d}"], M1[f"qd{d}"], M1["q"], MUL)
                TT(chunks(M1[f"ki{d}"]), chunks(M1[f"ki{d}"]), k4, MUL)
                ins = TT(chunks(M1[f"kd{d}"]), chunks(M1[f"kd{d}"]), k4, MUL)
            ins.then_inc(sems["lin_in"], 1)
            e.tiles("turn", 8)
            lin(M1, 2, 1, V("g_norm_a"), M1["tB"], P, lambda d, h: S0[:, d, h, :])
            u4 = kt(M1["u"], 4)
            for g in range(4):
                bank, free = ring_tile("turn")
                bs = M1["b_s"][:, g * P:(g + 1) * P].unsqueeze(1).broadcast_to([P, 2, P])
                TT(macc[:, 0, :].rearrange("p (t n) -> p t n", t=2), bank[:, 0:T].rearrange("p (t n) -> p t n", t=2), bs, ADD
                   ).then_inc(free, 1)
                dve.wait_ge(*e.tile_out())
                ins = TT(u4[:, g, :], u4[:, g, :], macc[:, 0, :], MUL)
                if g < 3:
                    ins.then_inc(sems["dve_step"], 1)
                    dve.wait_ge(sems["dve_step"], e.stepped())
            ins.then_inc(sems["sgu"], 1)
            mg, sgb = kt(M1["fg0"], 8), Hc
            for k in range(KT):
                bank, free = ring_tile("proj")
                TT(mg[:, k, :], bank[:, 0:T], ctxT[:, k, :], MUL).then_inc(free, 1)
            for k in range(KT):
                bank, free = ring_tile("proj")
                TT(sgb[:, k, :], bank[:, 0:T], sgb[:, k, :], MUL).then_inc(free, 1)
                dve.wait_ge(*e.tile_out())
                ins = TT(mg[:, k, :], mg[:, k, :], sgb[:, k, :], ADD)
            ins.then_inc(sems["merged"], 1)
            residual("proj", 16)
            make_gain(0, 32, V("g_ffn"))
            norm(xT, hT, gain[:, 0, :], True)
            hf = kt(M2["hf"], FT)
            sil = M2["sil"].rearrange("p (b j t) -> p b j t", b=2, j=2)
            for n in range(FT // 2):
                e.tiles("proj", 2)
                dve.wait_ge(*e.tile_out())
                for j in range(2):
                    bank, free = ring_tile("proj")
                    TT(hf[:, 2 * n + j, :], bank[:, 0:T], sil[:, n % 2, j, :], MUL).then_inc(free, 1)
            residual("turn", 40)
            norm(xT, xT, V("g_final"), False)
            used(8 + 22 + 11)
            dve.wait_ge(sems["h"], 4)
            mod_stage(24, 16, V("mod_b_2")[:, 0:48])
            STT(gain[:, 0, :], modc[:, 8:16], 1.0, V("norm_g_2")[:, 0:8], ADD, MUL).then_inc(sems["modulated"], 1)
            dve.wait_ge(sems["modulated"], 1)
            norm(xT, hT, gain[:, 0, :], True)
            e.tiles("turn", 5)
            dve.wait_ge(sems["zln"], e.more("zln"))
            STT(M3["cum0"], M3["zA"], 0.0, M3["zB"], ALU.min, SUB).then_inc(sems["dve_step"], 1)
            dve.wait_ge(sems["dve_step"], e.stepped())
            c4 = kt(M3["cum0"], 4)
            for h in range(4):
                ins = dve.tensor_tensor_scan(c4[:, h, :], C("scan_g"), c4[:, h, :], 0.0, MUL, ADD)
            ins.then_inc(sems["dve_step"], 1)
            dve.wait_ge(sems["dve_step"], e.stepped())
            x4 = chunks(M3["cum0"])
            TT(chunks(M3["tA"]), x4[:, :, :, CHUNK - 1:CHUNK].broadcast_to([P, 4, NCH, CHUNK]), x4, SUB).then_inc(sems["expo"], 1)
            dve.memset(M3["sc"], 0.0).then_inc(sems["dve_step"], 1)
            dve.wait_ge(sems["dve_step"], e.stepped())
            e.tiles("proj", 8 + 8 + 8)
            dve.wait_ge(sems["exps"], e.more("exps"))
            TT(M3["qi0"], M3["qi0"], M3["q"], MUL)
            TT(M3["ki0"], M3["ki0"], M3["k"], MUL)
            TT(M3["kd0"], M3["kd0"], M3["k"], MUL).then_inc(sems["lin_in"], 1)
            e.tiles("turn", 4)
            lin(M3, 1, 2, V("gla_norm_g"), M3["zA"], 2 * P, lambda d, h: None)
            residual("proj", 16)
            used(16)
            peer(0)
            mod_stage(8, 16, V("kv_mod_b"))
            STT(gain[:, 0, :], modc[:, 8:16], 1.0, V("kv_norm_g"), ADD, MUL).then_inc(sems["modulated"], 1)
            dve.wait_ge(sems["modulated"], 2)
            norm(xT, hT, gain[:, 0, :], True)
            used(3)
            dve.wait_ge(sems["pos_in"], e.more("pos_in", 32))
            ang, nn, tmp = M4["ang"][:, 0:T], M4["ang"][:, T:2 * T], M4["ang"][:, 2 * T:3 * T]
            dve.tensor_copy(tmp, M4["pos"].bitcast(i32)).then_inc(sems["dve_step"], 1)
            dve.wait_ge(sems["dve_step"], e.stepped())
            TS(ang, tmp, C("inv_freq"), None, MUL).then_inc(sems["dve_step"], 1)
            dve.wait_ge(sems["dve_step"], e.stepped())
            magic = 12582912.0
            TS(nn, ang, float(1 / (2 * np.pi)), magic, MUL, ADD).then_inc(sems["dve_step"], 1)
            dve.wait_ge(sems["dve_step"], e.stepped())
            TS(nn, nn, magic, None, SUB).then_inc(sems["dve_step"], 1)
            dve.wait_ge(sems["dve_step"], e.stepped())
            c1, c2 = 6.28125, float(np.float32(np.round((2 * np.pi - 6.28125) * 2 ** 20) / 2 ** 20))
            for c in (c1, c2, float(2 * np.pi - c1 - c2)):
                STT(ang, nn, -c, ang, MUL, ADD).then_inc(sems["dve_step"], 1)
                dve.wait_ge(sems["dve_step"], e.stepped())
            TS(ang, ang, float(np.float32(3.1415925)), float(np.float32(-3.1415925)), ALU.min, ALU.max).then_inc(sems["dve_step"], 1)
            dve.wait_ge(sems["dve_step"], e.stepped())
            TS(tmp, ang, -1.0, None, MUL).then_inc(sems["dve_step"], 1)
            dve.wait_ge(sems["dve_step"], e.stepped())
            TT(nn, ang, tmp, ALU.max).then_inc(sems["trig"], 1)
            e.tiles("proj", 6)
            dve.wait_ge(*e.tile_out())
            vP = M4["vP"].rearrange("p (n s c) -> p n s c", n=8, s=2)
            dve.memset(M4["vP"], 0.0).then_inc(sems["dve_step"], 1)
            dve.wait_ge(sems["dve_step"], e.stepped())
            for s in range(2):
                ins = dve.tensor_copy(vP[:, :, s, 64 * s:64 * s + 64], M4["vS"].rearrange("p (n c) -> p n c", n=8))
            ins.then_inc(sems["vpad"], 1)
            mod_stage(24, 16, V("mod_b_2")[:, 48:96])
            STT(gain[:, 0, :], modc[:, 8:16], 1.0, V("norm_g_2")[:, 16:24], ADD, MUL).then_inc(sems["modulated"], 1)
            dve.wait_ge(sems["modulated"], 3)
            norm(xT, hT, gain[:, 0, :], True)
            e.tiles("proj", 8)
            dve.wait_ge(sems["rope_in"], e.more("rope_in"))
            kS, qS, tR = kt(M4["kS"], 4), kt(M4["qS"], 8), M4["tR"].rearrange("p (b t) -> p b t", b=2)
            for n in range(12):
                dst = kS[:, n, :] if n < 4 else qS[:, n - 4, :]
                bank, free = ring_tile("turn")
                TT(tR[:, 0, :], bank[:, 0:T], M4["sinT"], MUL).then_inc(free, 1)
                TT(dst, dst, M4["cosT"], MUL).then_inc(sems["dve_step"], 1)
                dve.wait_ge(sems["dve_step"], e.stepped())
                dve.wait_ge(*e.tile_out())
                ins = TT(dst, dst, tR[:, 0, :], ADD)
                if n < 11:
                    ins.then_inc(sems["dve_step"], 1)
                    dve.wait_ge(sems["dve_step"], e.stepped())
            ins.then_inc(sems["roped"], 1)
            sS = M4["sS"].rearrange("p (b n) -> p b n", b=2)
            pS = M4["pS"].rearrange("p (b n) -> p b n", b=2)
            am = M4["am"].rearrange("p (b n) -> p b n", b=2)

            def att_max(h):
                b, sink = h % 2, V("sinks")[:, h:h + 1]
                dve.wait_ge(sems["att_s"], e.more("att_s"))
                STT(sS[:, b, :], BK[b][:, 0:3 * P], 0.125, M4["band"], MUL, ADD).then_inc(sems["att_sfree"], 1)
                dve.wait_ge(sems["att_sfree"], h + 1)
                dve.tensor_reduce(am[:, b, 0:1], sS[:, b, 0:P], AX.X, ALU.max)
                dve.tensor_reduce(am[:, b, 1:2], sS[:, b, P:3 * P], AX.X, ALU.max).then_inc(sems["dve_step"], 1)
                dve.wait_ge(sems["dve_step"], e.stepped())
                TS(am[:, b, 2:4], am[:, b, 0:2], sink, -1.0, ALU.max, MUL).then_inc(sems["dve_step"], 1)
                dve.wait_ge(sems["dve_step"], e.stepped())
                TS(am[:, b, 4:6], am[:, b, 2:4], sink, None, ADD).then_inc(sems["att_max"], 1)

            def att_div(h):
                b = h % 2
                dve.wait_ge(sems["att_exp"], e.more("att_exp"))
                TT(am[:, b, 8:10], am[:, b, 6:8], am[:, b, 4:6], ADD).then_inc(sems["dve_step"], 1)
                dve.wait_ge(sems["dve_step"], e.stepped())
                dve.reciprocal(am[:, b, 10:12], am[:, b, 8:10]).then_inc(sems["dve_step"], 1)
                dve.wait_ge(sems["dve_step"], e.stepped())
                TS(pS[:, b, 0:P], pS[:, b, 0:P], am[:, b, 10:11], None, MUL)
                TS(pS[:, b, P:3 * P], pS[:, b, P:3 * P], am[:, b, 11:12], None, MUL).then_inc(sems["att_p"], 1)

            att_max(0)
            for h in range(16):
                if h + 1 < 16:
                    att_max(h + 1)
                att_div(h)
            e.tiles("turn", 16)
            residual("proj", 16)
            used(8)
            peer(1)
            norm(xT, xT, V("final_norm_g"), False)

        @block.gpsimd
        def _(pool):
            e = Counts(sems)

            pool.dma_start(subT, a["subT"][0]).then_inc(sems["sub_in"], 16)
            pool.wait_ge(sems["modulated"], 1)
            pool.dma_start(wgl, a["gla_gl"]).then_inc(sems["wgl_in"], 16)
            pool.dma_start(M3["wg2"][0:16, :], a["gla_wg2"]).then_inc(sems["wg2_in"], 16)
            pool.wait_ge(sems["modulated"], 2)
            pool.dma_start(M4["pos"].bitcast(i32), a["pos"]).then_inc(sems["pos_in"], 16)
            pool.dma_start(M4["band"], a["band"]).then_inc(sems["pos_in"], 16)
            pool.wait_ge(sems["g_bank1"], 32)
            pool.dma_start(subT, a["subT"][1]).then_inc(sems["sub_in"], 16)


def kernel(**inputs):
    import concourse.bacc as _bacc
    from concourse.bass_utils import run_bass_kernel_spmd as _run

    def x(name):
        return np.asarray(inputs[name])

    def col_panels(w, cols=256):
        k, n = w.shape
        return np.ascontiguousarray(w.reshape(k // P, P, n // cols, cols).transpose(2, 1, 0, 3)).reshape(n // cols, P, SLOT)

    def columns(v):
        return np.asarray(v).reshape(-1, P).T

    vecs = {"c": x("c"), "c_ctx": x("c_ctx"), "c_2": x("c_2"), "b_mod": x("b_mod"), "g_mix": x("g_mix"), "g_ffn": x("g_ffn"),
            "g_final": x("g_final"), "lb_gamma": x("lb_gamma"), "g_norm_a": x("g_norm_a"), "mod_b_2": x("mod_b_2"),
            "norm_g_2": x("norm_g_2"), "gla_b_g2": x("gla_b_g2_2"), "gla_norm_g": x("gla_norm_g_2"),
            "kv_mod_b": x("kv_mod_b_2"), "kv_norm_g": x("kv_norm_g_2"), "final_norm_g": x("final_norm_g_2")}
    parts = []
    for name, size in VEC_SIZES:
        if name in vecs:
            parts.append(columns(vecs[name]))
        else:
            parts.append(np.broadcast_to(x("swa_sinks_2").reshape(1, 16), (P, 16)))
    iota = np.arange(P)
    scan = np.ones((2, P, 2 * T), np.float32)
    scan[0, :, 0] = 0
    scan[0, :, T::CHUNK] = 0
    scan[1, :, T - 1] = 0
    scan[1, :, T + CHUNK - 1::CHUNK] = 0
    rot = np.zeros((P, P), np.float32)
    inv = np.zeros((P, 1), np.float32)
    freq = (np.float32(500000.0) ** (-np.arange(0, 16, 2, dtype=np.float32) / np.float32(16))).astype(np.float32)
    for b in (0, 64):
        for i in range(8):
            rot[b + i + 8, b + i] = -1.0
            rot[b + i, b + i + 8] = 1.0
            inv[b + i] = inv[b + i + 8] = freq[i]
    q, k = iota[:, None], iota[None, :]
    no = np.float32(-1e30)
    own = np.where(k <= q, np.float32(0), no)
    prev = np.where(k > q, np.float32(0), no)
    cons = {"ident": np.eye(P), "ones": np.ones((P, P)), "iota": np.broadcast_to(iota, (P, P)), "rot": rot,
            "scan_g": scan[0][:, T:], "inv_freq": inv,
            "half_pi": np.full((P, 1), np.pi / 2)}
    s, t = np.arange(P)[:, None] % CHUNK, np.arange(CHUNK)[None, :]
    masks = np.stack([np.stack([s <= t] * 2, 1), np.stack([s >= t] * 2, 1)], 1).astype(np.int32)

    gla = x("gla_w_in_2")[0]
    kv = x("kv_w_2")
    kdup = np.concatenate([kv[:, g * 64:(g + 1) * 64] for g in range(4) for _ in range(2)], 1)
    w_up = x("w_up")[0].reshape(D, 2, FF // 256, 256).transpose(0, 2, 1, 3).reshape(D, 2 * FF)
    arrays = {
        "vec": np.concatenate(parts, 1).astype(np.float32),
        "con": np.concatenate([np.asarray(cons[n], np.float32) for n, _ in CONST_SIZES], 1),
        "masks": masks, "band": np.concatenate([own, prev, own], 1),
        "mix": np.concatenate([scan[0], scan[1]] + [np.broadcast_to(x(n).reshape(1, 512), (P, 512)) for n in ("ln_v_g", "ln_v_b", "b_s")], 1),
        "xT": x("x")[0].T.reshape(KT, P, T).transpose(1, 0, 2),
        "ctxT": x("ctx")[0].T.reshape(KT, P, T).transpose(1, 0, 2),
        "wsT": x("w_s")[0].transpose(2, 0, 1),
        "w_mod": col_panels(x("w_mod")[0]), "w_in": col_panels(x("w_in")[0]),
        "w_pab": np.concatenate([col_panels(x("w_pa")[0], 512), col_panels(x("w_pb")[0], 512)]),
        "w_o": col_panels(x("w_o")[0]), "w_up": col_panels(w_up),
        "w_down": x("w_down")[0].reshape(FT // 2, 2, P, D).transpose(0, 2, 1, 3).reshape(FT // 2, P, SLOT),
        "mod_w0": col_panels(x("mod_w_2")[0]), "mod_w1": col_panels(x("mod_w_2")[1]),
        "gla_qk": col_panels(gla[:, 0:1024]), "gla_v": col_panels(gla[:, 1024:2048]), "gla_og": col_panels(gla[:, 2048:3072]),
        "gla_gl": gla[:, 3072:].reshape(KT, P, 16).transpose(1, 0, 2), "gla_wg2": x("gla_w_g2_2")[0],
        "gla_out": col_panels(x("gla_w_out_2")[0]),
        "peer_wq": np.stack([col_panels(x("peer_w_q_2")[l]) for l in range(2)]),
        "subT": x("peer_subkeys_2").transpose(0, 3, 1, 2),
        "peer_u": np.stack([col_panels(x("peer_u_2")[l].T) for l in range(2)]),
        "peer_v": x("peer_v_2").reshape(2, 64, 2, P, D).transpose(0, 1, 3, 2, 4).reshape(2, 64, P, SLOT),
        "kv_mod": col_panels(x("kv_mod_w_2")), "kv_k": col_panels(kdup), "kv_v": col_panels(kv[:, 256:512]),
        "swa_q": col_panels(x("swa_w_q_2")[0]), "swa_out": col_panels(x("swa_w_out_2")[0]),
        "pos": np.broadcast_to(x("positions_2").reshape(1, T), (P, T)),
    }
    nc = _bacc.Bacc("TRN2", target_bir_lowering=False, num_devices=1)
    feed, aps = {}, {}
    for name, v in arrays.items():
        v = np.ascontiguousarray(v)
        feed[f"in_{name}"] = v
        aps[name] = nc.dram_tensor(f"in_{name}", v.shape, mybir.dt.from_np(v.dtype), kind="ExternalInput").ap()
    out = nc.dram_tensor("out_0", (1, T, D), mybir.dt.float32, kind="ExternalOutput").ap()
    build(nc, aps, out)
    r = _run(nc, [feed], core_ids=[0])
    return r.results[0]["out_0"]
```

```python
from contextlib import ExitStack

import numpy as np
from concourse import bass, mybir

D, T, P, KT = 1024, 256, 128, 8
FF = 2816
FT = FF // P
HEADS, CHUNK, NCH = 4, 64, 4
RING = 4
SLOT = 2048
EXPERTS, PH, TOPK = 16384, 8, 16
EPS = 1e-6
PAIRS = EXPERTS // (2 * P)

VEC_SIZES = [("c", 8), ("c_ctx", 8), ("c_2", 8), ("b_mod", 48), ("g_mix", 8), ("g_ffn", 8), ("g_final", 8),
             ("lb_gamma", 16), ("g_norm_a", 1), ("mod_b_2", 96), ("norm_g_2", 32), ("gla_b_g2", 4),
             ("gla_norm_g", 2), ("kv_mod_b", 16), ("kv_norm_g", 8), ("final_norm_g", 8),
             ("sinks", 16)]
VEC, _n = {}, 0
for _name, _size in VEC_SIZES:
    VEC[_name] = (_n, _n + _size)
    _n += _size
VEC_COLS = _n
CONST_SIZES = [("ident", 128), ("ones", 128), ("iota", 128), ("rot", 128), ("scan_g", 256), ("inv_freq", 1), ("half_pi", 1)]
CON, _n = {}, 0
for _name, _size in CONST_SIZES:
    CON[_name] = (_n, _n + _size)
    _n += _size
CON_COLS = _n
MIX_SIZES = [("scan_f", 512), ("scan_b", 512), ("ln_v_g", 512), ("ln_v_b", 512), ("b_s", 512)]


class Counts:

    def __init__(self, sems):
        self.sems = sems
        self.seen, self.fills, self.tile, self.steps = {}, {}, 0, 0
        self.i, self.rates = None, {}

    def value(self, name, n):
        return n if self.i is None or name not in self.rates else n + self.i * self.rates[name]

    def skip(self, name, n):
        self.seen[name] = self.seen.get(name, 0) + n

    def more(self, name, n=1):
        self.skip(name, n)
        return self.value(name, self.seen[name])

    def refill(self, name):
        self.fills[name] = self.fills.get(name, 0) + 1
        return self.fills[name] > 1

    def freed(self, name):
        return self.value(name, self.fills[name] - 1)

    def stepped(self):
        self.steps += 1
        return self.value("dve_step", self.steps)

    def tiles(self, name, n):
        self.tile += n
        self.skip(name, n)

    def tile_out(self, back=1):
        n = self.tile - back
        name = f"bank{4 + n % 2}"
        return self.sems[name], self.value(name, n // 2 + 1)

    def loop(self, i, rates):
        self.i, self.rates = i, rates

    def end_loop(self, times):
        for name, rate in self.rates.items():
            if name == "dve_step":
                self.steps += rate * (times - 1)
            if name in self.seen:
                self.seen[name] += rate * (times - 1)
            if name in self.fills:
                self.fills[name] += rate * (times - 1)
        self.i, self.rates = None, {}


def build(nc, a, out):
    f32, u32, i32 = mybir.dt.float32, mybir.dt.uint32, mybir.dt.int32
    ALU, ACT, AX = mybir.AluOpType, mybir.ActivationFunctionType, mybir.AxisListType
    MUL, ADD, SUB = ALU.mult, ALU.add, ALU.subtract
    ctx = ExitStack()
    with ctx:
        def sb(name, shape, dt=f32):
            return ctx.enter_context(nc.sbuf_tensor(name, shape, dt))

        ctx_at = -(-nc.sbuf_base // 32) * 32
        ctxT = sb("ctxT", [P, KT, T])
        h_at = nc.sbuf_base
        H = sb("H", [P, KT, 2 * T])
        ring_at = nc.sbuf_base
        ring = sb("ring", [P, RING, SLOT])
        xT = sb("xT", [P, KT, T])
        f32r = mybir.dt.float32r
        h_split = nc.alloc_sbuf_tensor_at("h_split", [P, 2, KT, T], f32r, offset=h_at)
        t_split = nc.alloc_sbuf_tensor_at("t_split", [P, 2, 2, SLOT // 2], f32r, offset=ring_at + 2 * SLOT * 4)
        w_split = nc.alloc_sbuf_tensor_at("w_split", [P, 2, 2, T], f32r, offset=ctx_at + 1024 * 4)
        vec = sb("vec", [P, VEC_COLS])
        con = sb("con", [P, CON_COLS])
        masks = sb("masks", [P, 2, 2, CHUNK], i32)
        small = sb("small", [P, 768])
        wsT = small[:, 0:512].rearrange("p (g t) -> p g t", g=4)
        subT = small[:, 512:768].rearrange("p (s n) -> p s n", s=2)
        modc = sb("modc", [P, 64])
        cact = sb("cact", [P, 24])
        gain = sb("gain", [P, 2, 8])
        lbs = sb("lbs", [P, 2, 8])
        nrm = sb("nrm", [P, 2, T])
        macc = sb("macc", [P, 3, T])
        arena = sb("arena", [P, 32768])

        def V(name):
            return vec[:, VEC[name][0]:VEC[name][1]]

        def C(name):
            return con[:, CON[name][0]:CON[name][1]]

        def slot(n):
            return ring[:, n % RING, :]

        def cut(sizes):
            at, views = 0, {}
            for name, size in sizes:
                views[name] = arena[:, at:at + size]
                at += size
            assert at <= 32768, at
            return views

        def kt(ap, k=KT):
            return ap.rearrange("p (k t) -> p k t", k=k)

        hT = H[:, :, :].rearrange("p k t -> p (k t)")[:, 0:KT * T].rearrange("p (k t) -> p k t", k=KT)
        Hc, Hx = H[:, :, 0:T], H[:, :, T:2 * T]
        ident, ones, iota = C("ident"), C("ones"), C("iota")
        BK = [ctx.enter_context(nc.psum_tensor(f"bank{i}", [P, 512], f32)) for i in range(8)]

        NAMES = (["consts_in", "x_in", "sub_in", "wgl_in", "pos_in", "wg2_in", "cact", "act_step", "dve_step", "pool_step", "mod_acc",
                  "mod_step", "mod_turn", "mod_bank", "proj", "turn", "bank4", "bank5", "sq", "ms", "var", "std", "h", "h_hi", "h_split", "hi", "split",
                  "lb", "gate", "gates_f", "logf", "expo", "exps", "lin_in", "kturn", "scores", "masked", "scores_free",
                  "dstate", "state", "dstate_free", "o_sum", "o_bank0", "o_bank1", "o_out", "osq", "oms", "ovar", "ostd",
                  "o_done", "wctx", "wctx_in", "s0", "s0_in", "vproj", "vln", "mixed", "mixed_free", "sgu", "merged", 
                  "rows", "y_out", "y_in", "out_done", "final", "gl", "glc", "sp_a", "sp_b", "sp_c",
                  "trig", "roped", "rope_in", "kv_ready", "att_s", "att_max", "att_exp", "att_p", "att_pt", "att_o", "att_bank0", "att_bank1",
                  "q_ready", "peer_top", "peer_sm", "peer_ex", "routes", "routes_in", "p2", "p_free", "g_mm", "g_bank0", "g_bank1",
                  "gelu", "w_ready", "w_free0", "w_free1", "zeroed", "vpad", "att_sfree", "hs", "x_new", "vvar", "vstd", "modulated", "wexp", "cums", "zeroed2", "xexp", "zexp", "zln", "att_sum"]
                 + [f"loaded{i}" for i in range(RING)])
        sems = {n: ctx.enter_context(nc.semaphore(n)) for n in NAMES}
        block = ctx.enter_context(nc.Block())

        M1 = cut([("fg0", 2048), ("fg1", 2048), ("cum0", 2048), ("cum1", 2048),
                  ("qi0", 1024), ("qi1", 1024), ("ki0", 1024), ("ki1", 1024), ("qd0", 1024), ("qd1", 1024),
                  ("kd0", 1024), ("kd1", 1024), ("tA", 1024), ("tB", 1024), ("q", 1024), ("og", 1024), ("u", 1024),
                  ("vN", 2048), ("vS", 1024), ("sc", 1024), ("kN", 512), ("St", 1536), ("S0", 1024),
                  ("oT", 1024), ("dec", 32), ("stat", 32)] + MIX_SIZES)
        mix_in = arena[:, 31808 - 2048:31808 - 2048 + 2560]
        W_ = {0: M1["qi0"], 1: M1["qi1"]}
        M2 = cut([("hf", FT * T), ("sil", 1024), ("yN", 2048)])
        M3 = cut([("cum0", 1024), ("qi0", 1024), ("ki0", 1024), ("kd0", 1024), ("tA", 1024), ("q", 1024), ("k", 1024),
                  ("og", 2048), ("vN", 2048), ("sc", 1024), ("kN", 512), ("St", 1536), ("oT", 2048), ("dec", 32),
                  ("glT", 256), ("zA", 1024), ("zB", 1024), ("wg2", 512), ("osq", 2048), ("wgl", 128)])
        wgl = M3["wgl"].rearrange("p (k r) -> p k r", k=8)
        M4 = cut([("kS", 1024), ("vS", 512), ("vP", 2048), ("cosT", 256), ("sinT", 256), ("qS", 2048), ("tR", 512),
                  ("sS", 768), ("pS", 768), ("pT", 768), ("oS", 2048), ("am", 64), ("ang", 1024), ("pos", 256), ("band", 384)])
        M5 = cut([("qT", 4096), ("s2", 256), ("topv", 512), ("topi", 512), ("topif", 512), ("cand", 256), ("cand2", 256),
                  ("cv", 256), ("ci", 256), ("ca", 256), ("cb", 256), ("caf", 256), ("cbf", 256), ("sel", 768),
                  ("eq", 2048), ("sm", 64), ("hP", 2048)])
        G = arena[:, :].rearrange("p (i t) -> p i t", i=P)
        yN = arena[:, 0:2048].rearrange("p (a d) -> p a d", a=2)
        cflat = ctxT[:, :, :].rearrange("p k t -> p (k t)")
        gelu_t = cflat[:, 0:512].rearrange("p (b t) -> p b t", b=2)
        w_t = cflat[:, 512:1024].rearrange("p (b t) -> p b t", b=2)
        routes = cflat[:, 1024:1792].rearrange("p (r t) -> p r t", r=3)
        P1 = ring[:, 2, 0:1024].rearrange("p (b j n) -> p b j n", b=2, j=4)
        P2 = ring[:, 2, 1024:2048].rearrange("p (b j n) -> p b j n", b=2, j=4)
        hP = M5["hP"].rearrange("p (k t) -> p k t", k=KT)

        def kview(m, h, d, dirs):
            v = m["kN"][:, 0:512].rearrange("p (d t n) -> p d t n", d=2, t=2)
            return v[:, d if dirs == 2 else h % 2, :, :]

        def state(m, h, d, r, dirs, E):
            v = m["St"].rearrange("p (b r n) -> p b r n", b=4 if dirs == 2 else 2, r=3)
            return v[:, (2 * d + h % 2) if dirs == 2 else h % 2, r, :]

        def chunks(ap, k=4):
            return ap.rearrange("p (h c t) -> p h c t", h=k, c=NCH)

        def xpart(cum):
            return cum.rearrange("p (h s t) -> p h s t", h=4, s=2 * NCH)[:, :, NCH:2 * NCH, :]

        fg = [M1["fg0"].rearrange("p (h t) -> p h t", h=4), M1["fg1"].rearrange("p (h t) -> p h t", h=4)]
        cum = [M1["cum0"].rearrange("p (h t) -> p h t", h=4), M1["cum1"].rearrange("p (h t) -> p h t", h=4)]

        def peer_sections(l):
            return [(a["peer_wq"][l], 8, "proj", 2), ((a["peer_u"][l], a["peer_v"][l]), 2 * PAIRS, None, 0)]

        SECTIONS = ([(a["w_mod"], 8, "mod_acc", 1)]
                    + [(a["w_in"], 1, "proj", 2), (a["w_mod"], 2, "mod_acc", 1)] * 4
                    + [(a["w_in"], 1, "proj", 4), (a["w_mod"], 2, "mod_acc", 1)] * 2
                    + [(a["w_in"], 1, "proj", 2), (a["w_mod"], 1, "mod_acc", 1)] * 4
                    + [(a["w_in"], 12, "proj", 2), (a["w_pab"], 4, "proj", 4), (a["w_o"], 4, "proj", 2)]
                    + [(a["w_up"], 2, "proj", 2), (a["mod_w0"], 2, "mod_acc", 1)] * (FT // 2)
                    + [(a["w_down"], 1, "rows", 1), (a["mod_w0"], 2, "mod_acc", 1), (a["w_down"], 10, "rows", 1),
                     (a["gla_qk"], 4, "proj", 2), (a["gla_v"], 4, "proj", 2), (a["gla_og"], 4, "proj", 2),
                     (a["gla_out"], 4, "proj", 2)]
                    + peer_sections(0)
                    + [(a["kv_mod"], 8, "mod_acc", 1), (a["kv_k"], 2, "proj", 2), (a["kv_v"], 1, "proj", 2),
                       (a["mod_w1"], 24, "mod_acc", 1), (a["swa_q"], 4, "proj", 2), (a["swa_out"], 4, "proj", 2)]
                    + peer_sections(1))
        LOADS_BEFORE, loads, n = [], [0, 0], 0
        for _, panels, signal, _ in SECTIONS:
            if signal is None:
                LOADS_BEFORE.append(list(loads))
                loads = [x + 16 * PAIRS for x in loads]
            else:
                for r in range(2):
                    loads[r] += 16 * sum(m % RING == r for m in range(n, n + panels))
                n += panels
        H_PEER = (6, 9)

        @block.sync
        def _(sync):
            e = Counts(sems)
            sync.dma_start(vec[:, :], a["vec"]).then_inc(sems["consts_in"], 16)
            sync.dma_start(con[:, :], a["con"]).then_inc(sems["consts_in"], 16)
            sync.dma_start(masks[:, :, :, :], a["masks"]).then_inc(sems["consts_in"], 16)
            sync.dma_start(xT[:, :, :], a["xT"]).then_inc(sems["x_in"], 16)
            sync.dma_start(ctxT[:, :, :], a["ctxT"]).then_inc(sems["x_in"], 16)
            sync.dma_start(wsT, a["wsT"]).then_inc(sems["x_in"], 16)
            sync.dma_start(mix_in, a["mix"]).then_inc(sems["x_in"], 16)
            n, freed, layer = 0, [], 0
            total = {"proj": 0, "mod_acc": 0, "rows": 0}
            at = {}

            def load(src):
                nonlocal n
                if n >= RING:
                    sync.wait_ge(sems[freed[n - RING][0]], freed[n - RING][1])
                sync.dma_start(slot(n), src).then_inc(sems[f"loaded{n % RING}"], 16)
                n += 1

            for dram, panels, signal, per in SECTIONS:
                if signal is not None:
                    k0 = at.get(id(dram), 0)
                    at[id(dram)] = k0 + panels
                    for k in range(panels):
                        total[signal] += per
                        freed.append((signal, total[signal]))
                        load(dram[k0 + k])
                    continue
                u, v = dram
                for r, table in ((0, u), (1, v)):
                    before = max(m for m in range(n) if m % RING == r)
                    sync.wait_ge(sems[freed[before][0]], freed[before][1])
                    sync.dma_start(ring[:, r, :], table[0]).then_inc(sems[f"loaded{r}"], 16)
                with sync.Fori(0, PAIRS - 1) as i:
                    for r, table in ((0, u), (1, v)):
                        sync.wait_ge(sems["split"], i * 4 + (4 * PAIRS * layer + 2 * r + 2))
                        sync.dma_start(ring[:, r, :], table[i + 1]).then_inc(sems[f"loaded{r}"], 16)
                layer += 1
                total["proj"] += 2 * PAIRS
                total["rows"] += PAIRS
                for m in range(n - RING, n):
                    freed[m] = ("rows", total["rows"])
            sync.wait_ge(sems["out_done"], 16)

        @block.tensor
        def _(pe):
            e = Counts(sems)
            mm = pe.matmul
            panel = [0]

            def next_panel():
                n = panel[0]
                pe.wait_ge(sems[f"loaded{n % RING}"], e.more(f"loaded{n % RING}", 16))
                panel[0] += 1
                return slot(n)

            def ring_bank():
                b = 4 + e.tile % 2
                if e.refill(f"bank{b}"):
                    pe.wait_ge(sems[f"bank{b}"], e.freed(f"bank{b}"))
                e.tile += 1
                return BK[b]

            def mod_stage(panels, ctx_panels=0):
                if e.refill("mod_bank"):
                    pe.wait_ge(sems["mod_bank"], e.freed("mod_bank"))

                def body(n, with_ctx):
                    for r in range(RING):
                        pe.wait_ge(sems["mod_acc"], e.more("mod_acc"))
                        for j in range(2):
                            c = (n + r) * 2 + j
                            last = mm(BK[6][:, bass.ds(c, 1)], macc[:, r % 2, j * P:(j + 1) * P], ones[:, 0:1], start=True, stop=True)
                        if with_ctx:
                            for j in range(2):
                                c = 48 + 2 * (n + r) + j
                                last = mm(BK[6][:, c:c + 1], macc[:, 2, j * P:(j + 1) * P], ones[:, 0:1], start=True, stop=True)
                        last.then_inc(sems["mod_turn"], 1)
                for n in range(0, ctx_panels, RING):
                    body(n, True)
                times = (panels - ctx_panels) // RING
                if times:
                    with pe.Fori(0, times) as i:
                        e.loop(i, {"mod_acc": RING})
                        body(i * RING + ctx_panels, False)
                        e.end_loop(times)
                panel[0] += panels
                for r in range(RING):
                    e.skip(f"loaded{r}", 16 * panels // RING)

            between = {"summed": 0, "turned": 0, "first": 0}

            def mod_start(first):
                if e.refill("mod_bank"):
                    pe.wait_ge(sems["mod_bank"], e.freed("mod_bank"))
                between.update(summed=0, turned=0, first=first)

            def mod_between(n):
                while between["turned"] < between["summed"]:
                    m = between["turned"]
                    pe.wait_ge(sems["mod_acc"], e.more("mod_acc"))
                    for j in range(2):
                        c = (between["first"] + m) * 2 + j
                        last = mm(BK[6][:, c:c + 1], macc[:, m % 2, j * P:(j + 1) * P], ones[:, 0:1], start=True, stop=True)
                    last.then_inc(sems["mod_turn"], 1)
                    between["turned"] += 1
                between["summed"] += n
                for _ in range(n):
                    e.skip(f"loaded{panel[0] % RING}", 16)
                    panel[0] += 1

            def norm(src):
                for k in range(KT):
                    pe.wait_ge(sems["sq"], e.more("sq"))
                    if k == 0:
                        if e.refill("var"):
                            pe.wait_ge(sems["var"], e.freed("var"))
                    last = mm(BK[7][:, 0:T], ones, src[:, k, :], start=(k == 0), stop=(k == KT - 1))
                last.then_inc(sems["ms"], 1)

            def proj_cols(panels, rhs, width, ks=KT, tiles=2, cols=P):
                for _ in range(panels):
                    w = next_panel().rearrange("p (k c) -> p k c", k=ks)
                    for j in range(tiles):
                        bank = ring_bank()
                        for k in range(ks):
                            last = mm(bank[:, 0:width], w[:, k, j * P:(j + 1) * P], rhs(k), start=(k == 0), stop=(k == ks - 1))
                        last.then_inc(sems["proj"], 1)

            def proj_rows(panels, lhs, tts):
                for _ in range(panels):
                    w = next_panel().rearrange("p (k c) -> p k c", k=KT)
                    for tt in range(tts):
                        bank = ring_bank()
                        for k in range(KT):
                            last = mm(bank[:, 0:2 * P], lhs(k, tt), w[:, k, :], start=(k == 0), stop=(k == KT - 1))
                        last.then_inc(sems["proj"], 1)

            def turn(src_list):
                bank = ring_bank()
                for n, s in enumerate(src_list):
                    last = pe.transpose(bank[:, n * P:(n + 1) * P], s, ident)
                last.then_inc(sems["turn"], 1)

            def lin_pre(m, h, dirs, E, vcols):
                for d in range(dirs):
                    kd = kt(m[f"kd{d}"], 4)
                    turn([kd[:, h, 0:P], kd[:, h, P:2 * P]])
                for d in range(dirs):
                    qi, ki = kt(m[f"qi{d}"], 4), kt(m[f"ki{d}"], 4)
                    for c in range(NCH):
                        tt, hf = c // 2, c % 2
                        s = slice(c * CHUNK, (c + 1) * CHUNK)
                        col = (2 * d + tt) * P + CHUNK * hf
                        last = mm(BK[h % 2][CHUNK * hf:CHUNK * hf + CHUNK, col:col + CHUNK], ki[:, h, s], qi[:, h, s],
                                  start=True, stop=True)
                last.then_inc(sems["scores"], 1)
                for d in range(dirs):
                    pe.wait_ge(*e.tile_out(dirs - d))
                    if e.refill("state"):
                        pe.wait_ge(sems["state"], e.freed("state"))
                    for r in range(3):
                        c = r if d == 0 else NCH - 1 - r
                        tt, hf = c // 2, c % 2
                        rows = slice(CHUNK * hf, CHUNK * hf + CHUNK)
                        b, col = BK[6 + c % 2], c // 2 * E * P
                        last = mm(b[:, col:col + E * P], kview(m, h, d, dirs)[rows, tt, :], vcols(tt, h)[rows, :],
                                  start=True, stop=True)
                    last.then_inc(sems["dstate"], 1)

            def lin_out(m, h, dirs, E, vcols, s0):
                pe.wait_ge(sems["masked"], e.more("masked"))
                if e.refill(f"o_bank{h % 2}"):
                    pe.wait_ge(sems[f"o_bank{h % 2}"], e.freed(f"o_bank{h % 2}"))
                o = BK[2 + h % 2]
                sc = m["sc"].rearrange("p (b q n) -> p b q n", b=2, q=4)
                first = True
                for x in range(E):
                    for d in range(dirs):
                        for tt in range(2):
                            mm(o[:, x * T + tt * P:x * T + tt * P + P], vcols(tt, h)[:, x * P:(x + 1) * P],
                               sc[:, h % 2, 2 * d + tt, :], start=first, stop=False, skip_group_check=True)
                            first = False
                for d in range(dirs):
                    pe.wait_ge(sems["state"], e.more("state"))
                last = None
                for x in range(E):
                    for d in range(dirs):
                        qd = kt(m[f"qd{d}"] if dirs == 2 else m["qi0"], 4)
                        for r in range(NCH):
                            c = r if d == 0 else NCH - 1 - r
                            if r == 0:
                                if s0 is None:
                                    continue
                                st = s0(d, h)
                            else:
                                st = state(m, h, d, r - 1, dirs, E)
                            last = mm(o[:, x * T + c * CHUNK:x * T + (c + 1) * CHUNK], st[:, x * P:(x + 1) * P],
                                      qd[:, h, c * CHUNK:(c + 1) * CHUNK], start=False, stop=(r == NCH - 1),
                                      skip_group_check=True)
                last.then_inc(sems["o_sum"], 1)

            def lin(m, dirs, E, vcols, s0):
                pe.wait_ge(sems["lin_in"], e.more("lin_in"))
                lin_pre(m, 0, dirs, E, vcols)
                for h in range(HEADS):
                    if h + 1 < HEADS:
                        lin_pre(m, h + 1, dirs, E, vcols)
                    lin_out(m, h, dirs, E, vcols, s0)
                osq = kt(m["osq"] if E == 2 else m["tA"], 4 * E)
                pe.wait_ge(sems["o_bank0"], e.more("o_bank0", 2))
                pe.wait_ge(sems["o_bank1"], e.more("o_bank1", 2))
                for pair in range(2):
                    for hh in range(2):
                        h = 2 * pair + hh
                        for x in range(E):
                            last = mm(BK[pair][:, hh * T:(hh + 1) * T], ones, osq[:, h * E + x, :],
                                      start=(x == 0), stop=(x == E - 1))
                last.then_inc(sems["oms"], 1)

            def rows_out(at_peer):
                pe.wait_ge(sems["y_out"], e.more("y_out"))
                y = (yN if at_peer else M2["yN"].rearrange("p (a d) -> p a d", a=2))
                for k in range(KT):
                    turn([y[:, tt, k * P:(k + 1) * P] for tt in range(2)])

            def peer(l):
                norm(hP)
                pe.wait_ge(sems["h"], e.more("h"))
                proj_cols(8, lambda k: hP[:, k, :], T)
                pe.wait_ge(sems["sub_in"], e.more("sub_in", 16))
                pe.wait_ge(*e.tile_out())
                qT = M5["qT"].rearrange("p (s t) -> p s t", s=16)
                for tt in range(2):
                    for h in range(PH):
                        bank = ring_bank()
                        for half in range(2):
                            last = mm(bank[:, half * P:(half + 1) * P], qT[:, 2 * h + half, tt * P:(tt + 1) * P],
                                      subT[:, half, :], start=True, stop=True)
                        last.then_inc(sems["turn"], 1)
                    pe.wait_ge(sems["routes"], e.more("routes"))
                    sel = M5["sel"].rearrange("p (b r n) -> p b r n", b=2, r=3)
                    bank = ring_bank()
                    for r in range(3):
                        last = pe.transpose(bank[:, r * P:(r + 1) * P], sel[:, tt, r, :], ident)
                    last.then_inc(sems["turn"], 1)
                def gates(first):
                    for b in range(2):
                        pe.wait_ge(sems["p2"], e.more("p2"))
                        if e.refill(f"g_bank{b}"):
                            pe.wait_ge(sems[f"g_bank{b}"], e.freed(f"g_bank{b}"))
                        for j in range(4):
                            last = mm(BK[6 + b][:, j * P:(j + 1) * P], P2[:, b, j, :], P1[:, b, j, :],
                                      start=True, stop=True)
                        last.then_inc(sems["g_mm"], 1)
                gates(True)
                with pe.Fori(0, 31) as i:
                    e.loop(i, {"p2": 2, "g_bank0": 1, "g_bank1": 1})
                    gates(False)
                    e.end_loop(31)

                pe.wait_ge(sems["h_split"], l + 1)

                def experts(first, last_one):
                    for j in range(2):
                        bank = ring_bank()
                        pe.wait_ge(sems["hi"], e.more("hi", 2))
                        u = t_split[:, j, :, :].rearrange("p s (k c) -> p s k c", k=KT)
                        for a_, b_ in ((0, 0), (0, 1), (1, 0)):
                            if a_ == 1:
                                pe.wait_ge(sems["split"], e.more("split"))
                            for k in range(KT):
                                last = mm(bank[:, 0:T], u[:, a_, k, :], h_split[:, b_, k, :],
                                          start=(k == 0 and a_ + b_ == 0), stop=(k == KT - 1 and a_ == 1))
                        last.then_inc(sems["proj"], 1)
                    for j in range(2):
                        pe.wait_ge(sems["hi"], e.more("hi", 2))
                        pe.wait_ge(sems["w_ready"], e.more("w_ready"))
                        for a_, b_ in ((0, 0), (1, 0), (0, 1)):
                            if b_ == 1:
                                pe.wait_ge(sems["split"], e.more("split"))
                            for tt in range(2):
                                for hf in range(2):
                                    last = mm(BK[2 * tt + hf][:, :], w_split[:, j, a_, tt * P:(tt + 1) * P],
                                              t_split[:, j, b_, hf * 512:(hf + 1) * 512],
                                              start=(first and j == 0 and a_ + b_ == 0), stop=(last_one and j == 1 and b_ == 1))
                        last.then_inc(sems["rows" if j else "w_free0"], 1)
                experts(True, False)
                with pe.Fori(0, PAIRS - 2) as i:
                    e.loop(i, {"hi": 8, "split": 4, "bank4": 1, "bank5": 1, "w_ready": 2})
                    experts(False, False)
                    e.end_loop(PAIRS - 2)
                experts(False, True)
                e.tile += 2 * (PAIRS - 3)
                for r in range(2):
                    e.skip(f"loaded{r}", 16 * PAIRS)
                rows_out(True)

            pe.wait_ge(sems["consts_in"], e.more("consts_in", 48))
            mod_stage(8, ctx_panels=8)
            norm(Hc)
            norm(Hx)
            pe.wait_ge(sems["h"], e.more("h", 2))
            mod_start(8)
            for _ in range(4):
                proj_cols(1, lambda k: H[:, k, :], 2 * T)
                mod_between(2)
            for _ in range(2):
                proj_rows(1, lambda k, tt: H[:, k, tt * P:(tt + 1) * P], 4)
                mod_between(2)
            for _ in range(4):
                proj_cols(1, lambda k: Hx[:, k, :], T)
                mod_between(1)
            proj_cols(1, lambda k: Hx[:, k, :], T)
            mod_between(0)
            proj_cols(1, lambda k: Hx[:, k, :], T)
            proj_rows(2, lambda k, tt: Hx[:, k, tt * P:(tt + 1) * P], 2)
            proj_cols(8, lambda k: Hx[:, k, :], T)
            vN1 = M1["vN"].rearrange("p (t n) -> p t n", t=4)
            for d in range(2):
                pe.wait_ge(sems["wctx"], e.more("wctx"))
                for h in range(HEADS):
                    w = kt(W_[d], 4)
                    turn([w[:, h, 0:P], w[:, h, P:2 * P]])
                    pe.wait_ge(*e.tile_out())
                    if e.refill("s0_in"):
                        pe.wait_ge(sems["s0_in"], e.freed("s0_in"))
                    kb = M1["kN"][:, 0:256].rearrange("p (t n) -> p t n", t=2)
                    for tt in range(2):
                        last = mm(BK[6][:, 0:P], kb[:, tt, :], vN1[:, tt, h * P:(h + 1) * P], start=(tt == 0), stop=(tt == 1))
                    last.then_inc(sems["s0"], 1)
            pe.wait_ge(sems["s0_in"], e.more("s0_in", 8))
            S0 = M1["S0"].rearrange("p (d h n) -> p d h n", d=2, h=4)
            lin(M1, 2, 1, lambda tt, h: vN1[:, 2 + tt, h * P:(h + 1) * P], lambda d, h: S0[:, d, h, :])
            pe.wait_ge(sems["vln"], e.more("vln", 1))
            pe.wait_ge(sems["x_in"], e.more("x_in", 64))
            vS = M1["vS"].rearrange("p (t n) -> p t n", t=2)
            for g in range(4):
                bank = ring_bank()
                for tt in range(2):
                    last = mm(bank[:, tt * P:(tt + 1) * P], vS[:, tt, g * P:(g + 1) * P], wsT[:, g, :], start=True, stop=True)
                last.then_inc(sems["turn"], 1)
            pe.wait_ge(sems["o_done"], e.more("o_done"))
            oT = kt(M1["oT"], 4)
            u4 = kt(M1["u"], 4)
            proj_cols(2, lambda k: oT[:, k, :], T, ks=4, tiles=4)
            pe.wait_ge(sems["sgu"], e.more("sgu"))
            proj_cols(2, lambda k: u4[:, k, :], T, ks=4, tiles=4)
            pe.wait_ge(sems["merged"], e.more("merged"))
            mg = kt(M1["fg0"], 8)
            proj_cols(4, lambda k: mg[:, k, :], T)
            norm(hT)
            pe.wait_ge(sems["h"], e.more("h"))
            mod_start(0)
            for _ in range(FT // 2):
                proj_cols(2, lambda k: hT[:, k, :], T)
                mod_between(2)
            pe.wait_ge(*e.tile_out())
            hf = kt(M2["hf"], FT)
            for n in range(FT // 2):
                w = next_panel().rearrange("p (j d) -> p j d", j=2)
                for j in range(2):
                    for tt in range(2):
                        for x in range(2):
                            last = mm(BK[2 * tt + x][:, :], hf[:, 2 * n + j, tt * P:(tt + 1) * P], w[:, j, x * 512:(x + 1) * 512],
                                      start=(n == 0 and j == 0), stop=(n == FT // 2 - 1 and j == 1))
                last.then_inc(sems["rows"], 1)
                if n in (0, 4):
                    mod_between(2 if n == 0 else 0)
            rows_out(False)
            norm(hT)
            e.skip("h", 1)
            norm(hT)
            pe.wait_ge(sems["h"], e.more("h"))
            pe.wait_ge(sems["wgl_in"], e.more("wgl_in", 16))
            bank = ring_bank()
            for k in range(KT):
                last = mm(bank[0:16, 0:T], wgl[:, k, :], hT[:, k, :], start=(k == 0), stop=(k == KT - 1))
            last.then_inc(sems["turn"], 1)
            pe.wait_ge(sems["wg2_in"], e.more("wg2_in", 16))
            pe.wait_ge(*e.tile_out())
            for h in range(HEADS):
                bank = ring_bank()
                mm(bank[:, 0:T], M3["wg2"][0:16, h * P:(h + 1) * P], M3["glT"][0:16, :], start=True, stop=True).then_inc(sems["turn"], 1)
            proj_cols(4, lambda k: hT[:, k, :], T)
            proj_rows(4, lambda k, tt: hT[:, k, tt * P:(tt + 1) * P], 2)
            proj_cols(4, lambda k: hT[:, k, :], T)
            vN3 = M3["vN"].rearrange("p (t n) -> p t n", t=2)
            lin(M3, 1, 2, lambda tt, h: vN3[:, tt, h * 2 * P:(h + 1) * 2 * P], None)
            pe.wait_ge(sems["o_done"], e.more("o_done"))
            o8 = kt(M3["oT"], 8)
            proj_cols(4, lambda k: o8[:, k, :], T)
            peer(0)
            mod_stage(8)
            norm(hT)
            pe.wait_ge(sems["h"], e.more("h"))
            proj_cols(2, lambda k: hT[:, k, :], T)
            proj_rows(1, lambda k, tt: hT[:, k, tt * P:(tt + 1) * P], 2)
            mod_stage(24)
            norm(hT)
            pe.wait_ge(sems["h"], e.more("h"))
            proj_cols(4, lambda k: hT[:, k, :], T)
            kS, qS = kt(M4["kS"], 4), kt(M4["qS"], 8)
            pe.wait_ge(*e.tile_out())
            for n in range(12):
                src = kS[:, n, :] if n < 4 else qS[:, n - 4, :]
                bank = ring_bank()
                mm(bank[:, 0:T], C("rot"), src, start=True, stop=True).then_inc(sems["turn"], 1)
            pe.wait_ge(sems["roped"], e.more("roped", 1))
            pS = M4["pS"].rearrange("p (b n) -> p b n", b=2)
            pT = M4["pT"].rearrange("p (b n) -> p b n", b=2)
            vP = M4["vP"].rearrange("p (t g s n) -> p t g s n", t=2, g=4, s=2)
            pe.wait_ge(sems["vpad"], e.more("vpad"))

            def att_scores(h):
                g, r = h // 4, slice(64 * (h % 2), 64 * (h % 2) + 64)
                b = BK[h % 2]
                q = qS[r, h // 2, :]
                if h >= 2:
                    pe.wait_ge(sems["att_sfree"], e.more("att_sfree"))
                mm(b[:, 0:P], q[:, 0:P], kS[r, g, 0:P], start=True, stop=True)
                mm(b[:, P:3 * P], q[:, P:2 * P], kS[r, g, 0:2 * P], start=True, stop=True).then_inc(sems["att_s"], 1)

            def att_out(h):
                pe.wait_ge(*e.tile_out())
                g, s, j = h // 4, h % 2, h // 2
                b = BK[2 + j % 2]
                if s == 0:
                    if e.refill(f"att_bank{j % 2}"):
                        pe.wait_ge(sems[f"att_bank{j % 2}"], e.freed(f"att_bank{j % 2}"))
                mm(b[:, 0:P], vP[:, 0, g, s, :], pT[:, h % 2, 0:P], start=(s == 0), stop=False, skip_group_check=True)
                mm(b[:, P:2 * P], vP[:, 0, g, s, :], pT[:, h % 2, P:2 * P], start=False, stop=False, skip_group_check=True)
                last = mm(b[:, P:2 * P], vP[:, 1, g, s, :], pT[:, h % 2, 2 * P:3 * P], start=False, stop=(s == 1), skip_group_check=True)
                last.then_inc(sems["att_o"], 1)

            att_scores(0)
            att_scores(1)
            for h in range(16):
                pe.wait_ge(sems["att_p"], e.more("att_p"))
                turn([pS[:, h % 2, n * P:(n + 1) * P] for n in range(3)])
                if h + 2 < 16:
                    att_scores(h + 2)
                att_out(h)
            pe.wait_ge(sems["att_bank0"], e.more("att_bank0", 4))
            pe.wait_ge(sems["att_bank1"], e.more("att_bank1", 4))
            oS = kt(M4["oS"], 8)
            proj_cols(4, lambda k: oS[:, k, :], T)
            peer(1)
            norm(hT)
            pe.wait_ge(sems["h"], e.more("h"))
            for tt in range(2):
                for x in range(2):
                    bank = ring_bank()
                    for j in range(4):
                        last = pe.transpose(bank[:, j * P:(j + 1) * P], xT[:, 4 * x + j, tt * P:(tt + 1) * P], ident)
                    last.then_inc(sems["turn"], 1)

        @block.scalar
        def _(act):
            e = Counts(sems)
            A = act.activation

            def evac(name, dst, func, width=T, split=None, **kw):
                b = 4 + e.tile % 2
                e.tile += 1
                act.wait_ge(sems[name], e.more(name))
                src = BK[b][:, 0:width]
                if split:
                    src = src.rearrange("p (t n) -> p t n", t=split)
                A(dst, src, func, **kw).then_inc(sems[f"bank{b}"], 1)

            def norm(src, dst, shift):
                for k in range(KT):
                    A(dst[:, k, :], src[:, k, :], ACT.Square).then_inc(sems["sq"], 1)
                act.wait_ge(sems["var"], e.more("var"))
                A(nrm[:, 1, :], nrm[:, 0, :], ACT.Sqrt).then_inc(sems["std"], 1)
                if shift is not None:
                    for k in range(KT):
                        act.wait_ge(sems["hs"], e.more("hs"))
                        last = A(dst[:, k, :], dst[:, k, :], ACT.Identity, bias=modc[:, shift + k:shift + k + 1])
                    last.then_inc(sems["h"], 1)

            def residual(name):
                e.tiles(name, 8)
                act.wait_ge(*e.tile_out())

            def rows_out(n, y):
                act.wait_ge(sems["rows"], e.more("rows", n))
                for tt in range(2):
                    for x in range(2):
                        last = A(y[:, tt, x * 512:(x + 1) * 512], BK[2 * tt + x][:, :], ACT.Copy)
                last.then_inc(sems["y_out"], 1)

            def lin(m, dirs, E, root_buf):
                oT, osq = kt(m["oT"], 4 * E), kt(m["osq"] if E == 2 else m["tA"], 4 * E)

                def turned(h):
                    for d in range(dirs):
                        evac("turn", kview(m, h, d, dirs), ACT.Copy, split=2)
                turned(0)
                for h in range(HEADS):
                    if h + 1 < HEADS:
                        turned(h + 1)
                    act.wait_ge(sems["o_sum"], e.more("o_sum"))
                    src = BK[2 + h % 2][:, 0:E * T].rearrange("p (x t) -> p x t", x=E)
                    A(oT[:, h * E:(h + 1) * E, :], src, ACT.Copy)
                    A(osq[:, h * E:(h + 1) * E, :], src, ACT.Square).then_inc(sems[f"o_bank{h % 2}"], 1)
                act.wait_ge(sems["ovar"], e.more("ovar"))
                A(root_buf, root_buf, ACT.Sqrt).then_inc(sems["ostd"], 1)

            def peer(l, scale_col, shift):
                norm(xT, hP, shift)
                act.wait_ge(sems["h"], H_PEER[l])
                A(h_split[:, 0, :, :], hP, ACT.Copy).then_inc(sems["h_hi"], 1)
                qT = M5["qT"].rearrange("p (s t) -> p s t", s=16)
                for s in range(16):
                    evac("proj", qT[:, s, :], ACT.Copy)
                for tt in range(2):
                    e.tiles("turn", 8)
                    act.wait_ge(sems["peer_sm"], e.more("peer_sm"))
                    A(M5["cv"][:, 0:128], M5["cv"][:, 0:128], ACT.Exp).then_inc(sems["peer_ex"], 1)
                    evac("turn", routes[:, :, tt * P:(tt + 1) * P], ACT.Copy, width=3 * P, split=3)

                def gates(at):
                    for b in range(2):
                        act.wait_ge(sems["g_mm"], e.more("g_mm"))
                        A(G[:, :, bass.ds(at + 4 * b, 4)].rearrange("p i t -> p t i"),
                          BK[6 + b][:, :].rearrange("p (t i) -> p t i", t=4), ACT.Copy).then_inc(sems[f"g_bank{b}"], 1)
                gates(0)
                with act.Fori(0, 31) as i:
                    e.loop(i, {"g_mm": 2})
                    gates(i * 8 + 8)
                    e.end_loop(31)

                def table(r):
                    act.wait_ge(sems[f"loaded{r}"], e.more(f"loaded{r}", 16))

                def hi(r, j):
                    view = "p (k j c) -> p j k c" if r == 0 else "p (j k c) -> p j k c"
                    tile = ring[:, r, :].rearrange(view, k=KT, j=2)[:, j]
                    for x in range(2):
                        A(t_split[:, j, 0, x * 512:(x + 1) * 512].rearrange("p (k c) -> p k c", k=4), tile[:, 4 * x:4 * x + 4, :],
                          ACT.Copy).then_inc(sems["hi"], 1)

                def gelu(j, first):
                    b = 4 + e.tile % 2
                    e.tile += 1
                    act.wait_ge(sems["proj"], e.more("proj"))
                    if not first:
                        act.wait_ge(sems["w_ready"], e.value("w_ready", 2 * PAIRS * l + 1 + j))
                    A(gelu_t[:, j, :], BK[b][:, 0:T], ACT.Gelu).then_inc(sems[f"bank{b}"], 1)

                def experts(first, last_one):
                    gelu(0, first)
                    table(1)
                    hi(1, 0)
                    gelu(1, first)
                    hi(1, 1)
                    if not last_one:
                        table(0)
                        act.wait_ge(sems["w_free0"], e.value("w_free0", PAIRS * l + 1 + (0 if first else 1)))
                        hi(0, 0)
                        act.wait_ge(sems["rows"], e.value("v_used", FT // 2 + PAIRS * l + 1 + (0 if first else 1)))
                        hi(0, 1)
                for r in range(2):
                    e.seen[f"loaded{r}"] = LOADS_BEFORE[l][r]
                table(0)
                hi(0, 0)
                hi(0, 1)
                experts(True, False)
                with act.Fori(0, PAIRS - 2) as i:
                    e.loop(i, {"proj": 2, "w_ready": 2, "loaded0": 16, "loaded1": 16, "w_free0": 1, "v_used": 1})
                    experts(False, False)
                    e.end_loop(PAIRS - 2)
                e.i, e.rates = PAIRS - 2, {"w_ready": 2}
                experts(False, True)
                e.i, e.rates = None, {}
                e.tile += 2 * (PAIRS - 3)
                rows_out(PAIRS, yN)
                residual("turn")

            act.wait_ge(sems["consts_in"], e.more("consts_in", 48))
            A(cact[:, 0:24], vec[:, 0:24], ACT.Silu).then_inc(sems["cact"], 1)
            act.wait_ge(sems["lb"], e.more("lb"))
            A(lbs[:, 0, :], lbs[:, 0, :], ACT.Sigmoid).then_inc(sems["gate"], 1)
            act.wait_ge(sems["x_in"], e.more("x_in", 64))
            norm(ctxT, Hc, 48)
            norm(xT, Hx, 0)
            for d in range(2):
                for h in range(4):
                    evac("proj", fg[d][:, h, :], ACT.Sigmoid, width=2 * T)
            vN1 = M1["vN"].rearrange("p (t n) -> p t n", t=4)
            for c in range(2):
                for tt in range(4):
                    evac("proj", vN1[:, tt, c * 2 * P:(c + 1) * 2 * P], ACT.Copy)
            for d in range(2):
                act.wait_ge(sems["gates_f"], e.more("gates_f"))
                A(cum[d], fg[d], ACT.Ln).then_inc(sems["logf"], 1)
            for h in range(4):
                evac("proj", kt(M1["q"], 4)[:, h, :], ACT.Copy)
            for h in range(4):
                evac("proj", kt(M1["og"], 4)[:, h, :], ACT.Silu)
            for h in range(4):
                evac("proj", kt(M1["u"], 4)[:, h, :], ACT.Gelu_apprx_tanh)
            vS1 = M1["vS"].rearrange("p (t n) -> p t n", t=2)
            for c in range(2):
                for tt in range(2):
                    evac("proj", vS1[:, tt, c * 2 * P:(c + 1) * 2 * P], ACT.Gelu_apprx_tanh)
            for k in range(KT):
                evac("proj", ctxT[:, k, :], ACT.Sigmoid)
            for k in range(KT):
                evac("proj", Hc[:, k, :], ACT.Sigmoid)
            act.wait_ge(sems["vvar"], e.more("vvar"))
            A(M1["stat"][:, 12:14], M1["stat"][:, 12:14], ACT.Sqrt).then_inc(sems["vstd"], 1)
            for d in range(2):
                act.wait_ge(sems["cums"], e.more("cums"))
                at = T - 1 if d == 0 else 0
                for h in range(4):
                    last = A(kt(W_[d], 4)[:, h, :], cum[d][:, h, 0:T], ACT.Exp, scale=-1.0, bias=cum[d][:, h, at:at + 1])
                last.then_inc(sems["wexp"], 1)
            for n in range(8):
                evac("turn", M1["kN"][:, 0:T], ACT.Copy)
            for d in range(2):
                act.wait_ge(sems["expo"], e.more("expo"))
                x4, t0 = xpart(M1[f"cum{d}"]), CHUNK - 1 if d == 0 else 0
                A(M1[f"qi{d}"], M1["tA"], ACT.Exp)
                A(M1[f"ki{d}"], M1["tA"], ACT.Exp, scale=-1.0)
                A(M1[f"kd{d}"], M1["tB"], ACT.Exp)
                A(chunks(M1[f"qd{d}"]), x4, ACT.Exp)
                A(M1["dec"][:, d * 16:(d + 1) * 16].rearrange("p (h c) -> p h c", h=4), x4[:, :, :, t0], ACT.Exp
                  ).then_inc(sems["exps"], 1)
            lin(M1, 2, 1, M1["tB"])
            e.tiles("turn", 4)
            e.tiles("proj", 16)
            residual("proj")
            norm(xT, hT, 24)
            sil = M2["sil"].rearrange("p (b j t) -> p b j t", b=2, j=2)
            for n in range(FT // 2):
                if n >= 2:
                    act.wait_ge(*e.tile_out(5))
                for j in range(2):
                    evac("proj", sil[:, n % 2, j, :], ACT.Silu)
                e.tiles("proj", 2)
            rows_out(FT // 2, M2["yN"].rearrange("p (a d) -> p a d", a=2))
            residual("turn")
            norm(xT, hT, None)
            act.wait_ge(sems["h"], 4)
            norm(xT, hT, 0)
            evac_gl = 4 + e.tile % 2
            e.tile += 1
            act.wait_ge(sems["turn"], e.more("turn"))
            A(M3["glT"][0:16, :], BK[evac_gl][0:16, 0:T], ACT.Copy).then_inc(sems[f"bank{evac_gl}"], 1)
            zA, zB = kt(M3["zA"], 4), kt(M3["zB"], 4)
            b0 = VEC["gla_b_g2"][0]
            for h in range(4):
                evac("turn", zA[:, h, :], ACT.Identity, bias=vec[:, b0 + h:b0 + h + 1])
            act.wait_ge(*e.tile_out())
            A(M3["zB"], M3["zA"], ACT.Abs).then_inc(sems["act_step"], 1)
            act.wait_ge(sems["act_step"], e.stepped())
            A(M3["zB"], M3["zB"], ACT.Exp, scale=-1.0).then_inc(sems["act_step"], 1)
            act.wait_ge(sems["act_step"], e.stepped())
            A(M3["zB"], M3["zB"], ACT.Ln, bias=ones[:, 0:1]).then_inc(sems["zln"], 1)
            for h in range(4):
                evac("proj", kt(M3["q"], 4)[:, h, :], ACT.Copy, scale=float(P) ** -0.5)
            for h in range(4):
                evac("proj", kt(M3["k"], 4)[:, h, :], ACT.Copy)
            vN3 = M3["vN"].rearrange("p (t n) -> p t n", t=2)
            for c in range(4):
                for tt in range(2):
                    evac("proj", vN3[:, tt, c * 2 * P:(c + 1) * 2 * P], ACT.Copy)
            for h in range(8):
                evac("proj", kt(M3["og"], 8)[:, h, :], ACT.Silu)
            act.wait_ge(sems["expo"], e.more("expo"))
            tau = 1.0 / 16.0
            A(M3["qi0"], M3["cum0"], ACT.Exp, scale=tau)
            A(M3["ki0"], M3["cum0"], ACT.Exp, scale=-tau)
            A(M3["kd0"], M3["tA"], ACT.Exp, scale=tau)
            A(M3["dec"][:, 0:16].rearrange("p (h c) -> p h c", h=4), chunks(M3["cum0"])[:, :, :, CHUNK - 1], ACT.Exp,
              scale=tau).then_inc(sems["exps"], 1)
            lin(M3, 1, 2, M3["zA"])
            residual("proj")
            peer(0, 32, 24)
            norm(xT, hT, 0)
            for g in range(4):
                evac("proj", kt(M4["kS"], 4)[:, g, :], ACT.Copy)
            for tt in range(2):
                evac("proj", M4["vS"].rearrange("p (t n) -> p t n", t=2)[:, tt, :], ACT.Copy)
            act.wait_ge(sems["trig"], e.more("trig"))
            A(M4["sinT"], M4["ang"][:, 0:T], ACT.Sin)
            A(M4["cosT"], M4["ang"][:, T:2 * T], ACT.Sin, scale=-1.0, bias=C("half_pi")).then_inc(sems["rope_in"], 1)
            norm(xT, hT, 0)
            for j in range(8):
                evac("proj", kt(M4["qS"], 8)[:, j, :], ACT.Copy)
            e.tiles("turn", 12)
            sS = M4["sS"].rearrange("p (b n) -> p b n", b=2)
            pS = M4["pS"].rearrange("p (b n) -> p b n", b=2)
            pT = M4["pT"].rearrange("p (b n) -> p b n", b=2)
            am = M4["am"].rearrange("p (b n) -> p b n", b=2)

            def att_exp(h):
                b = h % 2
                act.wait_ge(sems["att_max"], e.more("att_max"))
                A(pS[:, b, 0:P], sS[:, b, 0:P], ACT.Exp, bias=am[:, b, 2:3], accum_out=am[:, b, 6:7])
                A(pS[:, b, P:3 * P], sS[:, b, P:3 * P], ACT.Exp, bias=am[:, b, 3:4], accum_out=am[:, b, 7:8])
                A(am[:, b, 4:6], am[:, b, 4:6], ACT.Exp).then_inc(sems["att_exp"], 1)

            att_exp(0)
            for h in range(16):
                if h + 1 < 16:
                    att_exp(h + 1)
                evac("turn", pT[:, h % 2, :], ACT.Copy, width=3 * P)
                act.wait_ge(sems["att_o"], e.more("att_o"))
                if h % 2:
                    j = h // 2
                    A(kt(M4["oS"], 8)[:, j, :], BK[2 + j % 2][:, 0:T], ACT.Copy).then_inc(sems[f"att_bank{j % 2}"], 1)
            residual("proj")
            peer(1, 32, 24)
            norm(xT, hT, None)
            y = H[:, :, :].rearrange("p k t -> p (k t)")[:, 0:2048].rearrange("p (a d) -> p a d", a=2)
            for tt in range(2):
                for x in range(2):
                    evac("turn", y[:, tt, x * 512:(x + 1) * 512], ACT.Copy, width=512)
            act.wait_ge(*e.tile_out())
            act.dma_start(out.rearrange("o (a p) d -> p (o a) d", p=P), y).then_inc(sems["out_done"], 16)
            act.wait_ge(sems["out_done"], 16)

        @block.vector
        def _(dve):
            e = Counts(sems)
            TT, TS, STT = dve.tensor_tensor, dve.tensor_scalar, dve.scalar_tensor_tensor

            def ring_tile(name):
                b = 4 + e.tile % 2
                e.tile += 1
                dve.wait_ge(sems[name], e.more(name))
                return BK[b], sems[f"bank{b}"]

            panel = [0]
            mods = [0]

            def mod_stage(panels, c_col, bias, ctx_panels=0):
                def body(with_ctx, skip_first=False):
                    for r in range(RING):
                        dve.wait_ge(sems[f"loaded{(panel[0] + r) % RING}"], e.more(f"loaded{(panel[0] + r) % RING}", 16))
                        w = slot(panel[0] + r).rearrange("p (k c) -> p k c", k=KT)
                        if not (skip_first and r < 2):
                            dve.wait_ge(sems["mod_turn"], e.value("mod_turn", mods[0] - (0 if with_ctx else 1)))
                        elif with_ctx and r:
                            dve.wait_ge(sems["mod_turn"], mods[0])
                        mods[0] += 1
                        for which in ([1, 0] if with_ctx else [0]):
                            acc = macc[:, 2 if which else r % 2, :]
                            col = 8 if which else c_col
                            TS(acc, w[:, 0, :], cact[:, col:col + 1], None, MUL).then_inc(sems["dve_step"], 1)
                            dve.wait_ge(sems["dve_step"], e.stepped())
                            for k in range(1, KT):
                                ins = STT(acc, w[:, k, :], cact[:, col + k:col + k + 1], acc, MUL, ADD)
                                if which or k < KT - 1:
                                    ins.then_inc(sems["dve_step"], 1)
                                    dve.wait_ge(sems["dve_step"], e.stepped())
                        ins.then_inc(sems["mod_acc"], 1)
                for n in range(0, ctx_panels, RING):
                    body(True, n == 0 and mods[0] == 0)
                times = (panels - ctx_panels) // RING
                if times:
                    with dve.Fori(0, times) as i:
                        e.loop(i, {"dve_step": RING * (KT - 1), "mod_turn": RING, **{f"loaded{r}": 16 for r in range(RING)}})
                        body(False)
                        e.end_loop(times)
                    mods[0] += RING * (times - 1)
                panel[0] += panels
                mod_out(0, 2 * panels, bias, ctx_panels)

            def mod_between(n, c_col):
                for _ in range(n):
                    r, m = panel[0] % RING, mods[0]
                    panel[0] += 1
                    dve.wait_ge(sems[f"loaded{r}"], e.more(f"loaded{r}", 16))
                    w = ring[:, r, :].rearrange("p (k c) -> p k c", k=KT)
                    dve.wait_ge(sems["mod_turn"], m - 1)
                    mods[0] += 1
                    acc = macc[:, m % 2, :]
                    TS(acc, w[:, 0, :], cact[:, c_col:c_col + 1], None, MUL).then_inc(sems["dve_step"], 1)
                    dve.wait_ge(sems["dve_step"], e.stepped())
                    for k in range(1, KT):
                        ins = STT(acc, w[:, k, :], cact[:, c_col + k:c_col + k + 1], acc, MUL, ADD)
                        if k < KT - 1:
                            ins.then_inc(sems["dve_step"], 1)
                            dve.wait_ge(sems["dve_step"], e.stepped())
                    ins.then_inc(sems["mod_acc"], 1)

            def mod_out(first, cols, bias, ctx_panels=0):
                dve.wait_ge(sems["mod_turn"], mods[0])
                ins = TT(modc[:, first:first + cols], BK[6][:, first:first + cols], bias, ADD)
                if ctx_panels:
                    ins = TT(modc[:, 48:64], BK[6][:, 48:64], bias[:, 0:16], ADD)
                ins.then_inc(sems["mod_bank"], 1)
                dve.wait_ge(sems["mod_bank"], mod_uses[0] + 1)
                mod_uses[0] += 1

            mod_uses = [0]

            def used(n):
                for _ in range(n):
                    e.skip(f"loaded{panel[0] % RING}", 16)
                    panel[0] += 1

            def make_gain(i, scale, g):
                STT(gain[:, i, :], modc[:, scale:scale + 8], 1.0, g, ADD, MUL).then_inc(sems["dve_step"], 1)
                dve.wait_ge(sems["dve_step"], e.stepped())

            def norm(src, dst, g, shift):
                dve.wait_ge(sems["ms"], e.more("ms"))
                TS(nrm[:, 0, :], BK[7][:, 0:T], 1.0 / D, EPS, MUL, ADD).then_inc(sems["var"], 1)
                dve.wait_ge(sems["std"], e.more("std"))
                dve.reciprocal(nrm[:, 0, :], nrm[:, 1, :]).then_inc(sems["dve_step"], 1)
                dve.wait_ge(sems["dve_step"], e.stepped())
                for k in range(KT):
                    ins = STT(dst[:, k, :], src[:, k, :], g[:, k:k + 1], nrm[:, 0, :], MUL, MUL)
                    if shift:
                        ins.then_inc(sems["hs"], 1)
                if not shift:
                    ins.then_inc(sems["h"], 1)

            def residual(name, gate):
                for k in range(KT):
                    bank, free = ring_tile(name)
                    STT(xT[:, k, :], bank[:, 0:T], modc[:, gate + k:gate + k + 1], xT[:, k, :], MUL, ADD).then_inc(free, 1)
                dve.wait_ge(*e.tile_out())

            lins = [0, 0]

            def lin(m, dirs, E, g, root_buf, dv, s0):
                sc = m["sc"].rearrange("p (b q n) -> p b q n", b=2, q=4)
                oT = kt(m["oT"], 4 * E)
                for h in range(HEADS):
                    dve.wait_ge(sems["scores"], e.more("scores"))
                    if h >= 2:
                        dve.wait_ge(sems["o_sum"], lins[0] + h - 1)
                    for d in range(dirs):
                        for hf in range(2):
                            rows, cols = slice(64 * hf, 64 * hf + 64), slice(64 * hf, 64 * hf + 64)
                            src = BK[h % 2][:, :].rearrange("p (q n) -> p q n", q=4)
                            ins = dve.copy_predicated(sc[rows, h % 2, 2 * d:2 * d + 2, cols],
                                                      masks[rows, d, :, :], src[rows, 2 * d:2 * d + 2, cols])
                    ins.then_inc(sems["masked"], 1)
                    for d in range(dirs):
                        dve.wait_ge(sems["dstate"], e.more("dstate"))
                        for r in range(3):
                            c = r if d == 0 else NCH - 1 - r
                            dec = m["dec"][:, d * 16 + h * 4 + c:d * 16 + h * 4 + c + 1]
                            b, col = BK[6 + c % 2], c // 2 * E * P
                            before = s0(d, h) if r == 0 else state(m, h, d, r - 1, dirs, E)
                            if before is None:
                                ins = dve.tensor_copy(state(m, h, d, r, dirs, E), b[:, col:col + E * P])
                            else:
                                ins = STT(state(m, h, d, r, dirs, E), before, dec, b[:, col:col + E * P], MUL, ADD)
                            if r < 2:
                                ins.then_inc(sems["dve_step"], 1)
                                dve.wait_ge(sems["dve_step"], e.stepped())
                        ins.then_inc(sems["state"], 1)
                lins[0] += HEADS
                dve.wait_ge(sems["oms"], e.more("oms"))
                for pair in range(2):
                    ins = TS(root_buf[:, pair * 512:(pair + 1) * 512], BK[pair][:, :], 1.0 / dv, EPS, MUL, ADD)
                ins.then_inc(sems["ovar"], 1)
                dve.wait_ge(sems["ostd"], e.more("ostd"))
                dve.reciprocal(root_buf, root_buf).then_inc(sems["dve_step"], 1)
                dve.wait_ge(sems["dve_step"], e.stepped())
                for h in range(HEADS):
                    for x in range(E):
                        ins = STT(oT[:, h * E + x, :], oT[:, h * E + x, :], g[:, x:x + 1], root_buf[:, h * T:(h + 1) * T], MUL, MUL)
                ins.then_inc(sems["dve_step"], 1)
                dve.wait_ge(sems["dve_step"], e.stepped())
                TT(m["oT"], m["oT"], m["og"], MUL).then_inc(sems["o_done"], 1)

            iota16 = iota[:, 0:16].unsqueeze(1).broadcast_to([P, P, 16])

            def peer(l):
                make_gain(0, 32, V("norm_g_2")[:, (2 * l + 1) * 8:(2 * l + 2) * 8])
                norm(xT, hP, gain[:, 0, :], True)
                dve.wait_ge(sems["h_hi"], e.more("h_hi"))
                TT(h_split[:, 1, :, :], hP, h_split[:, 0, :, :].bitcast(f32), SUB).then_inc(sems["h_split"], 1)
                e.tiles("proj", 16)
                topv = M5["topv"][:, 0:256].rearrange("p (h s k) -> p h s k", h=8, s=2)
                topi = M5["topi"][:, 0:256].bitcast(u32).rearrange("p (h s k) -> p h s k", h=8, s=2)
                topif = M5["topif"][:, 0:256].rearrange("p (h s k) -> p h s k", h=8, s=2)
                s2, cand, cand2 = M5["s2"], M5["cand"], M5["cand2"]
                cv = M5["cv"][:, 0:128].rearrange("p (h k) -> p h k", h=8)
                ci = M5["ci"][:, 0:128].bitcast(u32).rearrange("p (h k) -> p h k", h=8)
                sel = M5["sel"].rearrange("p (b r n) -> p b r n", b=2, r=3)
                eq = M5["eq"].rearrange("p (n a) -> p n a", a=16)
                low = -3.0e38

                def top16(src, rest, values, indices, freed):
                    dve.max(values[:, 0:8], src).then_inc(sems["dve_step"], 1)
                    dve.wait_ge(sems["dve_step"], e.stepped())
                    dve.max_index(indices[:, 0:8], values[:, 0:8], src)
                    ins = dve.match_replace(rest, values[:, 0:8], src, low)
                    if freed is None:
                        ins.then_inc(sems["dve_step"], 1)
                        dve.wait_ge(sems["dve_step"], e.stepped())
                    else:
                        ins.then_inc(freed, 1)
                        dve.wait_ge(*e.tile_out())
                    dve.max(values[:, 8:16], rest).then_inc(sems["dve_step"], 1)
                    dve.wait_ge(sems["dve_step"], e.stepped())
                    dve.max_index(indices[:, 8:16], values[:, 8:16], rest).then_inc(sems["dve_step"], 1)
                    dve.wait_ge(sems["dve_step"], e.stepped())

                for tt in range(2):
                    for h in range(PH):
                        bank, free = ring_tile("turn")
                        for half in range(2):
                            top16(bank[:, half * P:(half + 1) * P], s2[:, 0:P], topv[:, h, half, :], topi[:, h, half, :],
                                  free if half else None)
                    dve.tensor_copy(M5["topif"][:, 0:256], M5["topi"][:, 0:256].bitcast(u32))
                    for h in range(PH):
                        TT(cand.rearrange("p (a b) -> p a b", a=16), topv[:, h, 0, :].unsqueeze(2).broadcast_to([P, 16, 16]),
                                  topv[:, h, 1, :].unsqueeze(1).broadcast_to([P, 16, 16]), ADD).then_inc(sems["dve_step"], 1)
                        dve.wait_ge(sems["dve_step"], e.stepped())
                        top16(cand, cand2, cv[:, h, :], ci[:, h, :], None)
                    TT(M5["sm"][:, 0:8], cv[:, :, 0], cv[:, :, 0], ALU.max).then_inc(sems["dve_step"], 1)
                    dve.wait_ge(sems["dve_step"], e.stepped())
                    TT(cv, cv, M5["sm"][:, 0:8].unsqueeze(2).broadcast_to([P, 8, 16]), SUB).then_inc(sems["peer_sm"], 1)
                    cu = M5["ci"][:, 0:128].bitcast(u32)
                    TS(M5["ca"][:, 0:128].bitcast(u32), cu, 4, None, ALU.logical_shift_right)
                    TS(M5["cb"][:, 0:128].bitcast(u32), cu, 15, None, ALU.bitwise_and).then_inc(sems["dve_step"], 1)
                    dve.wait_ge(sems["dve_step"], e.stepped())
                    dve.tensor_copy(M5["caf"][:, 0:128], M5["ca"][:, 0:128].bitcast(u32))
                    dve.tensor_copy(M5["cbf"][:, 0:128], M5["cb"][:, 0:128].bitcast(u32)).then_inc(sems["dve_step"], 1)
                    dve.wait_ge(sems["dve_step"], e.stepped())
                    for half, place in enumerate(("caf", "cbf")):
                        TT(eq, M5[place][:, 0:128].unsqueeze(2).broadcast_to([P, P, 16]), iota16, ALU.is_equal).then_inc(sems["dve_step"], 1)
                        dve.wait_ge(sems["dve_step"], e.stepped())
                        e4 = M5["eq"].rearrange("p (h k a) -> p h k a", h=8, k=16)
                        TT(e4, e4, topif[:, :, half, :].unsqueeze(2).broadcast_to([P, 8, 16, 16]), MUL).then_inc(sems["dve_step"], 1)
                        dve.wait_ge(sems["dve_step"], e.stepped())
                        dve.tensor_reduce(sel[:, tt, half, :], eq, AX.X, ADD).then_inc(sems["dve_step"], 1)
                        dve.wait_ge(sems["dve_step"], e.stepped())
                    dve.wait_ge(sems["peer_ex"], e.more("peer_ex"))
                    dve.tensor_reduce(M5["sm"][:, 8:16], cv, AX.X, ADD).then_inc(sems["dve_step"], 1)
                    dve.wait_ge(sems["dve_step"], e.stepped())
                    dve.reciprocal(M5["sm"][:, 16:24], M5["sm"][:, 8:16]).then_inc(sems["dve_step"], 1)
                    dve.wait_ge(sems["dve_step"], e.stepped())
                    TT(sel[:, tt, 2, :].rearrange("p (h k) -> p h k", h=8), cv,
                       M5["sm"][:, 16:24].unsqueeze(2).broadcast_to([P, 8, 16]), MUL).then_inc(sems["routes"], 1)
                    e.tiles("turn", 1)
                dve.wait_ge(*e.tile_out())

                def onehots(first, at):
                    for b in range(2):
                        if not first:
                            dve.wait_ge(sems["g_mm"], e.value("g_mm", 64 * l + 1 + b))
                        for j in range(4):
                            t = at + 4 * b + j
                            TS(P2[:, b, j, :], iota, routes[:, 1, bass.ds(t, 1)], routes[:, 2, bass.ds(t, 1)], ALU.is_equal, MUL)
                        TT(P1[:, b, :, :], iota.unsqueeze(1).broadcast_to([P, 4, P]),
                           routes[:, 0, bass.ds(at + 4 * b, 4)].unsqueeze(2).broadcast_to([P, 4, P]), ALU.is_equal).then_inc(sems["p2"], 1)
                onehots(True, 0)
                with dve.Fori(0, 31) as i:
                    e.loop(i, {"g_mm": 2})
                    onehots(False, i * 8 + 8)
                    e.end_loop(31)
                dve.wait_ge(sems["g_bank0"], 32 * (l + 1))
                dve.wait_ge(sems["g_bank1"], 32 * (l + 1))

                def lo(r, j):
                    view = "p (k j c) -> p j k c" if r == 0 else "p (j k c) -> p j k c"
                    tile = ring[:, r, :].rearrange(view, k=KT, j=2)[:, j]
                    for x in range(2):
                        dve.wait_ge(sems["hi"], e.more("hi"))
                        part = slice(x * 512, (x + 1) * 512)
                        ins = TT(t_split[:, j, 1, part].rearrange("p (k c) -> p k c", k=4), tile[:, 4 * x:4 * x + 4, :],
                                 t_split[:, j, 0, part].rearrange("p (k c) -> p k c", k=4).bitcast(f32), SUB)
                    ins.then_inc(sems["split"], 1)

                def weight(j, first, at):
                    e.tile += 1
                    dve.wait_ge(*e.tile_out())
                    TT(w_t[:, j, :], gelu_t[:, j, :], G[:, bass.ds(at + j, 1), :].rearrange("p o t -> p (o t)"), MUL
                       ).then_inc(sems["dve_step"], 1)
                    dve.wait_ge(sems["dve_step"], e.stepped())
                    if not first:
                        name, base = ("rows", FT // 2) if j else ("w_free0", 0)
                        dve.wait_ge(sems[name], e.value(name, base + PAIRS * l + 1))
                    dve.tensor_copy(w_split[:, j, 0, :], w_t[:, j, :]).then_inc(sems["dve_step"], 1)
                    dve.wait_ge(sems["dve_step"], e.stepped())
                    TT(w_split[:, j, 1, :], w_t[:, j, :], w_split[:, j, 0, :].bitcast(f32), SUB).then_inc(sems["w_ready"], 1)

                def experts(first, last_one, at):
                    weight(0, first, at)
                    lo(1, 0)
                    weight(1, first, at)
                    lo(1, 1)
                    if not last_one:
                        lo(0, 0)
                        lo(0, 1)
                lo(0, 0)
                lo(0, 1)
                experts(True, False, 0)
                with dve.Fori(0, PAIRS - 2) as i:
                    e.loop(i, {"dve_step": 4, "bank4": 1, "bank5": 1, "w_free0": 1, "rows": 1, "hi": 8})
                    experts(False, False, i * 2 + 2)
                    e.end_loop(PAIRS - 2)
                e.i, e.rates = PAIRS - 2, {"w_free0": 1, "rows": 1, "bank4": 0}
                e.tile += 2 * (PAIRS - 3)
                experts(False, True, 2 * PAIRS - 2)
                e.i, e.rates = None, {}
                e.skip("proj", 128)
                used(8)
                e.skip("loaded0", 16 * PAIRS)
                e.skip("loaded1", 16 * PAIRS)
                residual("turn", 40)

            dve.wait_ge(sems["consts_in"], e.more("consts_in", 48))
            g = V("lb_gamma").rearrange("p (l n) -> p l n", l=2)
            TT(lbs[:, 0, :], g[:, 0, :], g[:, 1, :], SUB).then_inc(sems["lb"], 1)
            dve.wait_ge(sems["gate"], e.more("gate"))
            TS(lbs[:, 1, :], lbs[:, 0, :], -1.0, 1.0, MUL, ADD).then_inc(sems["dve_step"], 1)
            dve.wait_ge(sems["dve_step"], e.stepped())
            dve.wait_ge(sems["cact"], e.more("cact"))
            dve.wait_ge(sems["x_in"], e.more("x_in", 64))
            mod_stage(8, 0, V("b_mod")[:, 0:16], ctx_panels=8)
            make_gain(1, 56, V("g_mix"))
            make_gain(0, 8, V("g_mix"))
            norm(ctxT, Hc, gain[:, 1, :], True)
            norm(xT, Hx, gain[:, 0, :], True)
            for d in range(2):
                for _ in range(2):
                    used(1)
                    mod_between(2, 0)
                e.tiles("proj", 4)
                dve.wait_ge(*e.tile_out())
                for h in range(4):
                    n = d * 4 + h
                    ins = TS(fg[d][:, h, :], fg[d][:, h, :], lbs[:, 1, n:n + 1], lbs[:, 0, n:n + 1], MUL, ADD)
                ins.then_inc(sems["gates_f"], 1)
            for _ in range(2):
                used(1)
                mod_between(2, 0)
            for d in range(2):
                dve.wait_ge(sems["logf"], e.more("logf"))
                TS(fg[d], fg[d], -1.0, 1.0, MUL, ADD)
                for h in range(4):
                    if d == 0:
                        ins = dve.tensor_tensor_scan(cum[d][:, h, :], M1["scan_f"], cum[d][:, h, :], 0.0, MUL, ADD)
                    else:
                        ins = dve.tensor_tensor_scan(cum[d][:, h, ::-1], M1["scan_b"][:, ::-1], cum[d][:, h, ::-1], 0.0, MUL, ADD)
                ins.then_inc(sems["cums"], 1)
                dve.wait_ge(sems["cums"], d + 1)
            for _ in range(4):
                used(1)
                mod_between(1, 0)
            mod_out(16, 32, V("b_mod")[:, 16:48])
            used(2 + 2 + 8)
            e.tiles("proj", 8 + 12 + 4)
            dve.wait_ge(*e.tile_out())
            vS1 = M1["vS"].rearrange("p (t n) -> p t n", t=2)
            stat = M1["stat"]
            for tt in range(2):
                dve.bn_stats(stat[:, 0:6], vS1[:, tt, :]).then_inc(sems["dve_step"], 1)
                dve.wait_ge(sems["dve_step"], e.stepped())
                dve.bn_aggr(stat[:, 6 + 2 * tt:8 + 2 * tt], stat[:, 0:6]).then_inc(sems["dve_step"], 1)
                dve.wait_ge(sems["dve_step"], e.stepped())
            TS(stat[:, 12:14], stat[:, 7:10:2], EPS, None, ADD).then_inc(sems["vvar"], 1)
            dve.wait_ge(sems["vstd"], e.more("vstd"))
            dve.reciprocal(stat[:, 14:16], stat[:, 12:14]).then_inc(sems["dve_step"], 1)
            dve.wait_ge(sems["dve_step"], e.stepped())
            for tt in range(2):
                TS(vS1[:, tt, :], vS1[:, tt, :], stat[:, 6 + 2 * tt:7 + 2 * tt], stat[:, 14 + tt:15 + tt], SUB, MUL).then_inc(sems["dve_step"], 1)
                dve.wait_ge(sems["dve_step"], e.stepped())
                TT(vS1[:, tt, :], vS1[:, tt, :], M1["ln_v_g"], MUL).then_inc(sems["dve_step"], 1)
                dve.wait_ge(sems["dve_step"], e.stepped())
                ins = TT(vS1[:, tt, :], vS1[:, tt, :], M1["ln_v_b"], ADD)
            ins.then_inc(sems["vln"], 1)
            for d in range(2):
                dve.wait_ge(sems["wexp"], e.more("wexp"))
                TT(kt(W_[d], 4), kt(W_[d], 4), fg[d][:, :, 0:T], MUL).then_inc(sems["wctx"], 1)
            e.tiles("proj", 16)
            S0 = M1["S0"].rearrange("p (d h n) -> p d h n", d=2, h=4)
            for n in range(8):
                dve.wait_ge(sems["s0"], e.more("s0"))
                dve.tensor_copy(S0[:, n // 4, n % 4, :], BK[6][:, 0:P]).then_inc(sems["s0_in"], 1)
            e.tiles("turn", 8)
            dve.memset(M1["sc"], 0.0).then_inc(sems["dve_step"], 1)
            dve.wait_ge(sems["dve_step"], e.stepped())
            for d in range(2):
                x4, t0 = xpart(M1[f"cum{d}"]), CHUNK - 1 if d == 0 else 0
                last = x4[:, :, :, t0:t0 + 1].broadcast_to([P, 4, NCH, CHUNK])
                for h in range(4):
                    STT(chunks(M1["tA"])[:, h], last[:, h], -0.5, x4[:, h], MUL, ADD)
                TT(chunks(M1["tB"]), last, x4, SUB).then_inc(sems["expo"], 1)
                dve.wait_ge(sems["exps"], e.more("exps"))
                k4 = xpart(M1[f"fg{d}"])
                TT(M1[f"qi{d}"], M1[f"qi{d}"], M1["q"], MUL)
                TT(M1[f"qd{d}"], M1[f"qd{d}"], M1["q"], MUL)
                TT(chunks(M1[f"ki{d}"]), chunks(M1[f"ki{d}"]), k4, MUL)
                ins = TT(chunks(M1[f"kd{d}"]), chunks(M1[f"kd{d}"]), k4, MUL)
            ins.then_inc(sems["lin_in"], 1)
            e.tiles("turn", 8)
            lin(M1, 2, 1, V("g_norm_a"), M1["tB"], P, lambda d, h: S0[:, d, h, :])
            u4 = kt(M1["u"], 4)
            for g in range(4):
                bank, free = ring_tile("turn")
                bs = M1["b_s"][:, g * P:(g + 1) * P].unsqueeze(1).broadcast_to([P, 2, P])
                TT(macc[:, 0, :].rearrange("p (t n) -> p t n", t=2), bank[:, 0:T].rearrange("p (t n) -> p t n", t=2), bs, ADD
                   ).then_inc(free, 1)
                dve.wait_ge(*e.tile_out())
                ins = TT(u4[:, g, :], u4[:, g, :], macc[:, 0, :], MUL)
                if g < 3:
                    ins.then_inc(sems["dve_step"], 1)
                    dve.wait_ge(sems["dve_step"], e.stepped())
            ins.then_inc(sems["sgu"], 1)
            mg, sgb = kt(M1["fg0"], 8), Hc
            for k in range(KT):
                bank, free = ring_tile("proj")
                TT(mg[:, k, :], bank[:, 0:T], ctxT[:, k, :], MUL).then_inc(free, 1)
            for k in range(KT):
                bank, free = ring_tile("proj")
                TT(sgb[:, k, :], bank[:, 0:T], sgb[:, k, :], MUL).then_inc(free, 1)
                dve.wait_ge(*e.tile_out())
                ins = TT(mg[:, k, :], mg[:, k, :], sgb[:, k, :], ADD)
            ins.then_inc(sems["merged"], 1)
            residual("proj", 16)
            make_gain(0, 32, V("g_ffn"))
            norm(xT, hT, gain[:, 0, :], True)
            hf = kt(M2["hf"], FT)
            sil = M2["sil"].rearrange("p (b j t) -> p b j t", b=2, j=2)
            used(4 + 4)
            for n in range(FT // 2):
                used(2)
                e.tiles("proj", 2)
                dve.wait_ge(*e.tile_out())
                for j in range(2):
                    bank, free = ring_tile("proj")
                    TT(hf[:, 2 * n + j, :], bank[:, 0:T], sil[:, n % 2, j, :], MUL).then_inc(free, 1)
                mod_between(2, 16)
            used(1)
            mod_between(2, 16)
            used(10)
            residual("turn", 40)
            norm(xT, xT, V("g_final"), False)
            dve.wait_ge(sems["h"], 4)
            mod_out(0, 48, V("mod_b_2")[:, 0:48])
            STT(gain[:, 0, :], modc[:, 8:16], 1.0, V("norm_g_2")[:, 0:8], ADD, MUL).then_inc(sems["modulated"], 1)
            dve.wait_ge(sems["modulated"], 1)
            norm(xT, hT, gain[:, 0, :], True)
            e.tiles("turn", 5)
            dve.wait_ge(sems["zln"], e.more("zln"))
            STT(M3["cum0"], M3["zA"], 0.0, M3["zB"], ALU.min, SUB).then_inc(sems["dve_step"], 1)
            dve.wait_ge(sems["dve_step"], e.stepped())
            c4 = kt(M3["cum0"], 4)
            for h in range(4):
                ins = dve.tensor_tensor_scan(c4[:, h, :], C("scan_g"), c4[:, h, :], 0.0, MUL, ADD)
            ins.then_inc(sems["dve_step"], 1)
            dve.wait_ge(sems["dve_step"], e.stepped())
            x4 = chunks(M3["cum0"])
            TT(chunks(M3["tA"]), x4[:, :, :, CHUNK - 1:CHUNK].broadcast_to([P, 4, NCH, CHUNK]), x4, SUB).then_inc(sems["expo"], 1)
            dve.memset(M3["sc"], 0.0).then_inc(sems["dve_step"], 1)
            dve.wait_ge(sems["dve_step"], e.stepped())
            e.tiles("proj", 8 + 8 + 8)
            dve.wait_ge(sems["exps"], e.more("exps"))
            TT(M3["qi0"], M3["qi0"], M3["q"], MUL)
            TT(M3["ki0"], M3["ki0"], M3["k"], MUL)
            TT(M3["kd0"], M3["kd0"], M3["k"], MUL).then_inc(sems["lin_in"], 1)
            e.tiles("turn", 4)
            lin(M3, 1, 2, V("gla_norm_g"), M3["zA"], 2 * P, lambda d, h: None)
            residual("proj", 16)
            used(16)
            peer(0)
            mod_stage(8, 16, V("kv_mod_b"))
            STT(gain[:, 0, :], modc[:, 8:16], 1.0, V("kv_norm_g"), ADD, MUL).then_inc(sems["modulated"], 1)
            dve.wait_ge(sems["modulated"], 2)
            norm(xT, hT, gain[:, 0, :], True)
            used(3)
            dve.wait_ge(sems["pos_in"], e.more("pos_in", 32))
            ang, nn, tmp = M4["ang"][:, 0:T], M4["ang"][:, T:2 * T], M4["ang"][:, 2 * T:3 * T]
            dve.tensor_copy(tmp, M4["pos"].bitcast(i32)).then_inc(sems["dve_step"], 1)
            dve.wait_ge(sems["dve_step"], e.stepped())
            TS(ang, tmp, C("inv_freq"), None, MUL).then_inc(sems["dve_step"], 1)
            dve.wait_ge(sems["dve_step"], e.stepped())
            magic = 12582912.0
            TS(nn, ang, float(1 / (2 * np.pi)), magic, MUL, ADD).then_inc(sems["dve_step"], 1)
            dve.wait_ge(sems["dve_step"], e.stepped())
            TS(nn, nn, magic, None, SUB).then_inc(sems["dve_step"], 1)
            dve.wait_ge(sems["dve_step"], e.stepped())
            c1, c2 = 6.28125, float(np.float32(np.round((2 * np.pi - 6.28125) * 2 ** 20) / 2 ** 20))
            for c in (c1, c2, float(2 * np.pi - c1 - c2)):
                STT(ang, nn, -c, ang, MUL, ADD).then_inc(sems["dve_step"], 1)
                dve.wait_ge(sems["dve_step"], e.stepped())
            TS(ang, ang, float(np.float32(3.1415925)), float(np.float32(-3.1415925)), ALU.min, ALU.max).then_inc(sems["dve_step"], 1)
            dve.wait_ge(sems["dve_step"], e.stepped())
            TS(tmp, ang, -1.0, None, MUL).then_inc(sems["dve_step"], 1)
            dve.wait_ge(sems["dve_step"], e.stepped())
            TT(nn, ang, tmp, ALU.max).then_inc(sems["trig"], 1)
            e.tiles("proj", 6)
            dve.wait_ge(*e.tile_out())
            vP = M4["vP"].rearrange("p (n s c) -> p n s c", n=8, s=2)
            dve.memset(M4["vP"], 0.0).then_inc(sems["dve_step"], 1)
            dve.wait_ge(sems["dve_step"], e.stepped())
            for s in range(2):
                ins = dve.tensor_copy(vP[:, :, s, 64 * s:64 * s + 64], M4["vS"].rearrange("p (n c) -> p n c", n=8))
            ins.then_inc(sems["vpad"], 1)
            mod_stage(24, 16, V("mod_b_2")[:, 48:96])
            STT(gain[:, 0, :], modc[:, 8:16], 1.0, V("norm_g_2")[:, 16:24], ADD, MUL).then_inc(sems["modulated"], 1)
            dve.wait_ge(sems["modulated"], 3)
            norm(xT, hT, gain[:, 0, :], True)
            e.tiles("proj", 8)
            dve.wait_ge(sems["rope_in"], e.more("rope_in"))
            kS, qS, tR = kt(M4["kS"], 4), kt(M4["qS"], 8), M4["tR"].rearrange("p (b t) -> p b t", b=2)
            for n in range(12):
                dst = kS[:, n, :] if n < 4 else qS[:, n - 4, :]
                bank, free = ring_tile("turn")
                TT(tR[:, 0, :], bank[:, 0:T], M4["sinT"], MUL).then_inc(free, 1)
                TT(dst, dst, M4["cosT"], MUL).then_inc(sems["dve_step"], 1)
                dve.wait_ge(sems["dve_step"], e.stepped())
                dve.wait_ge(*e.tile_out())
                ins = TT(dst, dst, tR[:, 0, :], ADD)
                if n < 11:
                    ins.then_inc(sems["dve_step"], 1)
                    dve.wait_ge(sems["dve_step"], e.stepped())
            ins.then_inc(sems["roped"], 1)
            sS = M4["sS"].rearrange("p (b n) -> p b n", b=2)
            pS = M4["pS"].rearrange("p (b n) -> p b n", b=2)
            am = M4["am"].rearrange("p (b n) -> p b n", b=2)

            def att_max(h):
                b, sink = h % 2, V("sinks")[:, h:h + 1]
                dve.wait_ge(sems["att_s"], e.more("att_s"))
                STT(sS[:, b, :], BK[b][:, 0:3 * P], 0.125, M4["band"], MUL, ADD).then_inc(sems["att_sfree"], 1)
                dve.wait_ge(sems["att_sfree"], h + 1)
                dve.tensor_reduce(am[:, b, 0:1], sS[:, b, 0:P], AX.X, ALU.max)
                dve.tensor_reduce(am[:, b, 1:2], sS[:, b, P:3 * P], AX.X, ALU.max).then_inc(sems["dve_step"], 1)
                dve.wait_ge(sems["dve_step"], e.stepped())
                TS(am[:, b, 2:4], am[:, b, 0:2], sink, -1.0, ALU.max, MUL).then_inc(sems["dve_step"], 1)
                dve.wait_ge(sems["dve_step"], e.stepped())
                TS(am[:, b, 4:6], am[:, b, 2:4], sink, None, ADD).then_inc(sems["att_max"], 1)

            def att_div(h):
                b = h % 2
                dve.wait_ge(sems["att_exp"], e.more("att_exp"))
                TT(am[:, b, 8:10], am[:, b, 6:8], am[:, b, 4:6], ADD).then_inc(sems["dve_step"], 1)
                dve.wait_ge(sems["dve_step"], e.stepped())
                dve.reciprocal(am[:, b, 10:12], am[:, b, 8:10]).then_inc(sems["dve_step"], 1)
                dve.wait_ge(sems["dve_step"], e.stepped())
                TS(pS[:, b, 0:P], pS[:, b, 0:P], am[:, b, 10:11], None, MUL)
                TS(pS[:, b, P:3 * P], pS[:, b, P:3 * P], am[:, b, 11:12], None, MUL).then_inc(sems["att_p"], 1)

            att_max(0)
            for h in range(16):
                if h + 1 < 16:
                    att_max(h + 1)
                att_div(h)
            e.tiles("turn", 16)
            residual("proj", 16)
            used(8)
            peer(1)
            norm(xT, xT, V("final_norm_g"), False)

        @block.gpsimd
        def _(pool):
            e = Counts(sems)

            pool.dma_start(subT, a["subT"][0]).then_inc(sems["sub_in"], 16)
            pool.wait_ge(sems["modulated"], 1)
            pool.dma_start(wgl, a["gla_gl"]).then_inc(sems["wgl_in"], 16)
            pool.dma_start(M3["wg2"][0:16, :], a["gla_wg2"]).then_inc(sems["wg2_in"], 16)
            pool.wait_ge(sems["g_bank1"], 32)
            pool.dma_start(subT, a["subT"][1]).then_inc(sems["sub_in"], 16)
            pool.wait_ge(sems["modulated"], 2)
            pool.dma_start(M4["pos"].bitcast(i32), a["pos"]).then_inc(sems["pos_in"], 16)
            pool.dma_start(M4["band"], a["band"]).then_inc(sems["pos_in"], 16)


def kernel(**inputs):
    import concourse.bacc as _bacc
    from concourse.bass_utils import run_bass_kernel_spmd as _run

    def x(name):
        return np.asarray(inputs[name])

    def col_panels(w, cols=256):
        k, n = w.shape
        return np.ascontiguousarray(w.reshape(k // P, P, n // cols, cols).transpose(2, 1, 0, 3)).reshape(n // cols, P, SLOT)

    def columns(v):
        return np.asarray(v).reshape(-1, P).T

    vecs = {"c": x("c"), "c_ctx": x("c_ctx"), "c_2": x("c_2"), "b_mod": x("b_mod"), "g_mix": x("g_mix"), "g_ffn": x("g_ffn"),
            "g_final": x("g_final"), "lb_gamma": x("lb_gamma"), "g_norm_a": x("g_norm_a"), "mod_b_2": x("mod_b_2"),
            "norm_g_2": x("norm_g_2"), "gla_b_g2": x("gla_b_g2_2"), "gla_norm_g": x("gla_norm_g_2"),
            "kv_mod_b": x("kv_mod_b_2"), "kv_norm_g": x("kv_norm_g_2"), "final_norm_g": x("final_norm_g_2")}
    parts = []
    for name, size in VEC_SIZES:
        if name in vecs:
            parts.append(columns(vecs[name]))
        else:
            parts.append(np.broadcast_to(x("swa_sinks_2").reshape(1, 16), (P, 16)))
    iota = np.arange(P)
    scan = np.ones((2, P, 2 * T), np.float32)
    scan[0, :, 0] = 0
    scan[0, :, T::CHUNK] = 0
    scan[1, :, T - 1] = 0
    scan[1, :, T + CHUNK - 1::CHUNK] = 0
    rot = np.zeros((P, P), np.float32)
    inv = np.zeros((P, 1), np.float32)
    freq = (np.float32(500000.0) ** (-np.arange(0, 16, 2, dtype=np.float32) / np.float32(16))).astype(np.float32)
    for b in (0, 64):
        for i in range(8):
            rot[b + i + 8, b + i] = -1.0
            rot[b + i, b + i + 8] = 1.0
            inv[b + i] = inv[b + i + 8] = freq[i]
    q, k = iota[:, None], iota[None, :]
    no = np.float32(-1e30)
    own = np.where(k <= q, np.float32(0), no)
    prev = np.where(k > q, np.float32(0), no)
    cons = {"ident": np.eye(P), "ones": np.ones((P, P)), "iota": np.broadcast_to(iota, (P, P)), "rot": rot,
            "scan_g": scan[0][:, T:], "inv_freq": inv,
            "half_pi": np.full((P, 1), np.pi / 2)}
    s, t = np.arange(P)[:, None] % CHUNK, np.arange(CHUNK)[None, :]
    masks = np.stack([np.stack([s <= t] * 2, 1), np.stack([s >= t] * 2, 1)], 1).astype(np.int32)

    gla = x("gla_w_in_2")[0]
    kv = x("kv_w_2")
    kdup = np.concatenate([kv[:, g * 64:(g + 1) * 64] for g in range(4) for _ in range(2)], 1)
    w_up = x("w_up")[0].reshape(D, 2, FF // 256, 256).transpose(0, 2, 1, 3).reshape(D, 2 * FF)
    arrays = {
        "vec": np.concatenate(parts, 1).astype(np.float32),
        "con": np.concatenate([np.asarray(cons[n], np.float32) for n, _ in CONST_SIZES], 1),
        "masks": masks, "band": np.concatenate([own, prev, own], 1),
        "mix": np.concatenate([scan[0], scan[1]] + [np.broadcast_to(x(n).reshape(1, 512), (P, 512)) for n in ("ln_v_g", "ln_v_b", "b_s")], 1),
        "xT": x("x")[0].T.reshape(KT, P, T).transpose(1, 0, 2),
        "ctxT": x("ctx")[0].T.reshape(KT, P, T).transpose(1, 0, 2),
        "wsT": x("w_s")[0].transpose(2, 0, 1),
        "w_mod": col_panels(x("w_mod")[0]), "w_in": col_panels(x("w_in")[0]),
        "w_pab": np.concatenate([col_panels(x("w_pa")[0], 512), col_panels(x("w_pb")[0], 512)]),
        "w_o": col_panels(x("w_o")[0]), "w_up": col_panels(w_up),
        "w_down": x("w_down")[0].reshape(FT // 2, 2, P, D).transpose(0, 2, 1, 3).reshape(FT // 2, P, SLOT),
        "mod_w0": col_panels(x("mod_w_2")[0]), "mod_w1": col_panels(x("mod_w_2")[1]),
        "gla_qk": col_panels(gla[:, 0:1024]), "gla_v": col_panels(gla[:, 1024:2048]), "gla_og": col_panels(gla[:, 2048:3072]),
        "gla_gl": gla[:, 3072:].reshape(KT, P, 16).transpose(1, 0, 2), "gla_wg2": x("gla_w_g2_2")[0],
        "gla_out": col_panels(x("gla_w_out_2")[0]),
        "peer_wq": np.stack([col_panels(x("peer_w_q_2")[l]) for l in range(2)]),
        "subT": x("peer_subkeys_2").transpose(0, 3, 1, 2),
        "peer_u": np.stack([col_panels(x("peer_u_2")[l].T) for l in range(2)]),
        "peer_v": x("peer_v_2").reshape(2, 64, 2, P, D).transpose(0, 1, 3, 2, 4).reshape(2, 64, P, SLOT),
        "kv_mod": col_panels(x("kv_mod_w_2")), "kv_k": col_panels(kdup), "kv_v": col_panels(kv[:, 256:512]),
        "swa_q": col_panels(x("swa_w_q_2")[0]), "swa_out": col_panels(x("swa_w_out_2")[0]),
        "pos": np.broadcast_to(x("positions_2").reshape(1, T), (P, T)),
    }
    nc = _bacc.Bacc("TRN2", target_bir_lowering=False, num_devices=1)
    feed, aps = {}, {}
    for name, v in arrays.items():
        v = np.ascontiguousarray(v)
        feed[f"in_{name}"] = v
        aps[name] = nc.dram_tensor(f"in_{name}", v.shape, mybir.dt.from_np(v.dtype), kind="ExternalInput").ap()
    out = nc.dram_tensor("out_0", (1, T, D), mybir.dt.float32, kind="ExternalOutput").ap()
    build(nc, aps, out)
    r = _run(nc, [feed], core_ids=[0])
    return r.results[0]["out_0"]
```
